# Optimizing a Trainium2 kernel written in Bass

```python
import math
import jax, jax.numpy as jnp
from jax import lax
import numpy as np

D_MODEL = 1024
BATCH = 1
SEQ = 1024
DEPTH = 1

HEAD_DIM = 64
BLOCK = 128
WINDOW = 128
A_Q_HEADS = 8
A_KV_HEADS = 2
A_GROUP = A_Q_HEADS // A_KV_HEADS
B_HEADS = 8
N_BRANCHES = 2
ROPE_THETA = 10000.0
RMS_EPS = 1e-6
_ffn_raw = (8 * D_MODEL + 2) // 3
D_FF = ((_ffn_raw + 255) // 256) * 256

A_Q_W = A_Q_HEADS * HEAD_DIM
A_KV_W = A_KV_HEADS * HEAD_DIM
B_W = B_HEADS * HEAD_DIM
GATE_W = N_BRANCHES * D_MODEL
IN_SPLITS = [A_Q_W, A_KV_W, A_KV_W, B_W, B_W, B_W, B_HEADS, GATE_W]
IN_OFFSETS = list(np.cumsum(IN_SPLITS)[:-1])
IN_W = int(sum(IN_SPLITS))
N_ADA = 6

kernel_name = "hybrid_swa_sink_fox_gated_block"

def rms_norm(x, g):
    xf = x.astype(jnp.float32)
    y = xf * lax.rsqrt(jnp.mean(xf * xf, axis=-1, keepdims=True) + RMS_EPS)
    return (y * g.astype(jnp.float32)).astype(x.dtype)

def rope(x, positions):
    dh = x.shape[-1]
    inv_freq = 1.0 / (ROPE_THETA ** (jnp.arange(0, dh, 2, dtype=jnp.float32) / dh))
    ang = positions.astype(jnp.float32)[..., None] * inv_freq
    cos = jnp.cos(ang)[:, :, None, :]
    sin = jnp.sin(ang)[:, :, None, :]
    xf = x.astype(jnp.float32)
    x1, x2 = xf[..., : dh // 2], xf[..., dh // 2:]
    out = jnp.concatenate([x1 * cos - x2 * sin, x2 * cos + x1 * sin], axis=-1)
    return out.astype(x.dtype)

def sliding_window_gqa_sinks(q, k, v, sinks):
    B, S, _, dh = q.shape
    nb = S // BLOCK
    scale = 1.0 / math.sqrt(dh)
    qb = q.reshape(B, nb, BLOCK, A_KV_HEADS, A_GROUP, dh)
    pad = ((0, 0), (BLOCK, 0), (0, 0), (0, 0))
    kp = jnp.pad(k, pad).reshape(B, nb + 1, BLOCK, A_KV_HEADS, dh)
    vp = jnp.pad(v, pad).reshape(B, nb + 1, BLOCK, A_KV_HEADS, dh)
    kb = jnp.concatenate([kp[:, :-1], kp[:, 1:]], axis=2)
    vb = jnp.concatenate([vp[:, :-1], vp[:, 1:]], axis=2)
    s = jnp.einsum('bnqhgd,bnkhd->bnhgqk', qb, kb).astype(jnp.float32) * scale
    q_loc = jnp.arange(BLOCK) + BLOCK
    k_loc = jnp.arange(2 * BLOCK)
    rel = q_loc[:, None] - k_loc[None, :]
    band = (rel >= 0) & (rel < WINDOW)
    k_abs = jnp.arange(nb)[:, None] * BLOCK + k_loc[None, :] - BLOCK
    valid = band[None, :, :] & (k_abs >= 0)[:, None, :]
    s = jnp.where(valid[None, :, None, None], s, -jnp.inf)
    sink = sinks.astype(jnp.float32).reshape(1, 1, A_KV_HEADS, A_GROUP, 1, 1)
    m = jnp.maximum(jnp.max(s, axis=-1, keepdims=True), sink)
    p = jnp.exp(s - m)
    denom = jnp.sum(p, axis=-1, keepdims=True) + jnp.exp(sink - m)
    p = p / denom
    o = jnp.einsum('bnhgqk,bnkhd->bnqhgd', p, vb.astype(jnp.float32))
    return o.reshape(B, S, A_Q_HEADS * dh)

def forgetting_attention(q, k, v, log_f):
    B, S, H, dh = q.shape
    nb = S // BLOCK
    scale = 1.0 / math.sqrt(dh)
    cum = lax.cumsum(log_f, axis=1)
    cum_k = jnp.transpose(cum, (0, 2, 1))
    k_pos = jnp.arange(S)
    vf = v.astype(jnp.float32)

    def one_block(i):
        start = i * BLOCK
        qi = lax.dynamic_slice_in_dim(q, start, BLOCK, axis=1)
        ci = lax.dynamic_slice_in_dim(cum, start, BLOCK, axis=1)
        s = jnp.einsum('bqhd,bkhd->bhqk', qi, k).astype(jnp.float32) * scale
        s = s + jnp.transpose(ci, (0, 2, 1))[..., None] - cum_k[:, :, None, :]
        q_pos = start + jnp.arange(BLOCK)
        s = jnp.where((k_pos[None, :] <= q_pos[:, None])[None, None], s, -jnp.inf)
        p = jax.nn.softmax(s, axis=-1)
        return jnp.einsum('bhqk,bkhd->bqhd', p, vf)

    o = lax.map(one_block, jnp.arange(nb))
    return jnp.transpose(o, (1, 0, 2, 3, 4)).reshape(B, S, H * dh)

def setup_inputs(seed: int = 0) -> dict:
    key = jax.random.key(seed)
    ks = jax.random.split(key, 20)
    f32 = jnp.float32
    nrm = lambda k, shape, s: jax.random.normal(k, shape, f32) * s
    x = nrm(ks[0], (BATCH, SEQ, D_MODEL), 1.0)
    c = nrm(ks[1], (BATCH, D_MODEL), 1.0)
    positions = jnp.broadcast_to(jnp.arange(SEQ, dtype=jnp.int32), (BATCH, SEQ))
    w_ada = nrm(ks[2], (DEPTH, D_MODEL, N_ADA * D_MODEL), 0.5 * D_MODEL ** -0.5)
    b_ada = nrm(ks[3], (DEPTH, N_ADA * D_MODEL), 0.01)
    g_pre_mix = 1.0 + nrm(ks[4], (DEPTH, D_MODEL), 0.05)
    g_post_mix = 1.0 + nrm(ks[5], (DEPTH, D_MODEL), 0.05)
    w_in = nrm(ks[6], (DEPTH, D_MODEL, IN_W), D_MODEL ** -0.5)
    b_f = 1.0 + nrm(ks[7], (DEPTH, B_HEADS), 0.1)
    sinks = nrm(ks[8], (DEPTH, A_Q_HEADS), 0.5)
    w_branch_a = nrm(ks[9], (DEPTH, A_Q_W, D_MODEL), A_Q_W ** -0.5)
    w_branch_b = nrm(ks[10], (DEPTH, B_W, D_MODEL), B_W ** -0.5)
    w_out = nrm(ks[11], (DEPTH, D_MODEL, D_MODEL), D_MODEL ** -0.5)
    g_pre_ffn = 1.0 + nrm(ks[12], (DEPTH, D_MODEL), 0.05)
    g_post_ffn = 1.0 + nrm(ks[13], (DEPTH, D_MODEL), 0.05)
    w_ffn_in = nrm(ks[14], (DEPTH, D_MODEL, 2 * D_FF), D_MODEL ** -0.5)
    w_ffn_out = nrm(ks[15], (DEPTH, D_FF, D_MODEL), D_FF ** -0.5)
    return {"x": x, "c": c, "positions": positions, "w_ada": w_ada, "b_ada": b_ada,
            "g_pre_mix": g_pre_mix, "g_post_mix": g_post_mix, "w_in": w_in, "b_f": b_f,
            "sinks": sinks, "w_branch_a": w_branch_a, "w_branch_b": w_branch_b,
            "w_out": w_out, "g_pre_ffn": g_pre_ffn, "g_post_ffn": g_post_ffn,
            "w_ffn_in": w_ffn_in, "w_ffn_out": w_ffn_out}

def reference(x, c, positions, w_ada, b_ada, g_pre_mix, g_post_mix, w_in, b_f, sinks,
              w_branch_a, w_branch_b, w_out, g_pre_ffn, g_post_ffn, w_ffn_in, w_ffn_out):
    B, S, D = x.shape
    for l in range(DEPTH):
        ada = (c @ w_ada[l] + b_ada[l]).reshape(B, N_ADA, D)[:, :, None, :]
        shift_m, scale_m, gate_m = ada[:, 0], ada[:, 1], ada[:, 2]
        shift_f, scale_f, gate_f = ada[:, 3], ada[:, 4], ada[:, 5]

        h = rms_norm(x, g_pre_mix[l]) * (1.0 + scale_m) + shift_m
        proj = h @ w_in[l]
        qa, ka, va, qb, kb, vb, f_logit, gate_logit = jnp.split(proj, IN_OFFSETS, axis=-1)
        qa = rope(qa.reshape(B, S, A_Q_HEADS, HEAD_DIM), positions)
        ka = rope(ka.reshape(B, S, A_KV_HEADS, HEAD_DIM), positions)
        va = va.reshape(B, S, A_KV_HEADS, HEAD_DIM)
        o_a = sliding_window_gqa_sinks(qa, ka, va, sinks[l]).astype(x.dtype)

        log_f = jax.nn.log_sigmoid((f_logit + b_f[l]).astype(jnp.float32))
        o_b = forgetting_attention(qb.reshape(B, S, B_HEADS, HEAD_DIM),
                                   kb.reshape(B, S, B_HEADS, HEAD_DIM),
                                   vb.reshape(B, S, B_HEADS, HEAD_DIM), log_f).astype(x.dtype)

        gates = jax.nn.sigmoid(gate_logit).reshape(B, S, N_BRANCHES, D)
        merged = gates[:, :, 0] * (o_a @ w_branch_a[l]) + gates[:, :, 1] * (o_b @ w_branch_b[l])
        y = merged @ w_out[l]
        x = x + gate_m * rms_norm(y, g_post_mix[l])

        h = rms_norm(x, g_pre_ffn[l]) * (1.0 + scale_f) + shift_f
        gu = h @ w_ffn_in[l]
        g_part, u_part = gu[..., :D_FF], gu[..., D_FF:]
        y = (jax.nn.silu(g_part) * u_part) @ w_ffn_out[l]
        x = x + gate_f * rms_norm(y, g_post_ffn[l])
    return x


_drawn_inputs = setup_inputs


def setup_inputs(seed=0):
    import zlib

    import numpy as np

    out = dict(_drawn_inputs(seed))
    spreads = {}
    factors = {'b_ada': 3.299, 'b_f': 4.09, 'sinks': 8.0, 'g_post_ffn': 2.702}
    for name, (base, spread) in spreads.items():
        noise = np.random.default_rng([zlib.crc32(name.encode()), seed]).standard_normal(out[name].shape)
        drawn = base * np.exp(spread * noise) if base else spread * noise
        out[name] = __import__('jax').numpy.asarray(drawn.astype(out[name].dtype))
    for name, factor in factors.items():
        out[name] = (out[name] * factor).astype(out[name].dtype)
    return out
```

```python
from contextlib import ExitStack
import math

import concourse.bass as bass
from concourse import mybir

F32 = mybir.dt.float32
F32R = mybir.dt.float32r
BF16 = mybir.dt.bfloat16
I32 = mybir.dt.int32
ALU = mybir.AluOpType
ACT = mybir.ActivationFunctionType

P = 128
HALF = 64
NT = 512
EPS = 1e-6
BIG = 3.0e38
MASKED = -1.0e30
ROUND = 1.5 * 2.0 ** 23
TURN = (6.28125, 0.0019350051879882812, 3.019813448190689e-07, 1.0253376273028358e-11)
PI_BELOW = 3.1415925
BR_BANK = (4, 5, 6, 3)
TERMS = ((0, 0), (0, 1), (1, 0))


def hybrid_layer(nc, x, c, positions, w_ada, b_ada, g_pre_mix, g_post_mix, w_in, b_f, sinks,
                 w_branch_a, w_branch_b, w_out, g_pre_ffn, g_post_ffn, w_ffn_in, w_ffn_out,
                 inv_freq, out):
    S, D = x.shape[1], x.shape[2]
    NTOK = S // P
    KD = D // P
    CH = S // NT
    FT = w_ffn_out.shape[1] // P
    DFF = FT * P
    HD = HALF
    A_Q, A_KV, B_H = sinks.shape[1], 2, b_f.shape[1]
    C_QA = 0
    C_KA = C_QA + A_Q * HD
    C_VA = C_KA + A_KV * HD
    C_QB = C_VA + A_KV * HD
    C_KB = C_QB + B_H * HD
    C_VB = C_KB + B_H * HD
    C_F = C_VB + B_H * HD
    C_G = C_F + B_H
    VB_W, VA_W = B_H * HD, A_KV * HD
    WV = VB_W + B_H + VA_W
    SM = 1.0 / math.sqrt(HD)
    assert (S, D, HD, VB_W, A_Q, B_H) == (1024, 1024, 64, 512, 8, 8)

    oT_dram = nc.dram_tensor("oT_dram", (8, P, S), F32, kind="Internal").ap()
    x1_dram = nc.dram_tensor("x1_dram", (NTOK, P, D), F32, kind="Internal").ap()
    ncum_dram = nc.dram_tensor("ncum_dram", (B_H, S), F32, kind="Internal").ap()

    base = (nc.sbuf_base + 63) // 64 * 64
    KB = 1024

    def at(name, off, shape, dt=F32):
        return nc.alloc_sbuf_tensor_at(name, shape, dt, offset=base + off)

    cursor = [0]

    def small(name, shape, dt=F32):
        size = 2 if dt == BF16 else 4
        for n in shape[1:]:
            size *= n
        o = cursor[0]
        cursor[0] += (size + 31) // 32 * 32
        return at(name, o, shape, dt)

    ident = small("ident", [P, P])
    tri = small("tri", [P, P])
    ones = small("ones", [P, P])
    band = small("band", [P, 2 * P])
    identb = small("identb", [P, P], BF16)
    causalb = small("causalb", [P, P], BF16)
    pcols = small("pcols", [P, 88])
    adac = small("adac", [P, 48])
    a_mix = small("a_mix", [P, KD])
    a_ffn = small("a_ffn", [P, KD])
    gm_col = small("gm_col", [P, 2 * KD])
    invf = small("invf", [P, 1])
    sgn = small("sgn", [P, 1])
    bfb = small("bfb", [P, B_H])
    sinkb = small("sinkb", [P, A_Q])
    nsink = small("nsink", [P, A_Q])
    nmax = small("nmax", [P, 4])
    den = small("den", [P, 4])
    rden = small("rden", [P, 2])
    ot = small("ot", [P, 2, HALF])
    ssq = small("ssq", [P, 32])
    z = small("z", [P, NTOK, B_H])
    credit = small("credit", [P, 8])
    scratch = small("scratch", [P, 1])
    ssq_b = small("ssq_b", [P, NTOK])
    var = small("var", [P, 32])
    rms = small("rms", [P, 32])
    rstd = small("rstd", [P, 32])
    P_END = (cursor[0] + 63) // 64 * 64
    H0 = P_END
    W0 = H0 + 64 * KB
    R0 = W0 + 24 * KB
    R_SIZE = nc.sbuf_usable_end - base - R0
    assert R_SIZE >= int(128.5 * KB), R_SIZE

    act_hl = [at(f"act_{s}", H0 + i * 32 * KB, [P, KD, S], F32R) for i, s in enumerate(("hi", "lo"))]
    wraw = at("wraw", W0, [P, 2, KD, P])
    w_hl = [at(f"w_{s}", W0 + (1 + i) * 8 * KB, [P, 2, KD, P], F32R) for i, s in enumerate(("hi", "lo"))]
    wada = at("wada", R0, [P, 2, KD, NT])
    posi = at("posi", R0 + 32 * KB, [P, S], I32)
    ang = at("ang", R0 + 32 * KB, [P, S])
    turns = at("turns", R0 + 36 * KB, [P, S])
    wv_hl = [at(f"wv_{s}", R0 + 40 * KB + i * 4 * KD * WV, [P, KD, WV], F32R) for i, s in enumerate(("hi", "lo"))]
    wvraw = at("wvraw", W0, [P, KD, WV])
    XIN = 40 * KB + 8 * KD * WV
    xin = at("xin", R0 + XIN, [P, NTOK, D])
    CS = XIN + 32 * KB
    cs = at("cs", R0 + CS, [P, 2, 2, S])
    htmp = at("htmp", R0 + CS + 8 * KB, [P, 2, NT])
    junk = at("junk", R0 + CS + 12 * KB, [P, D])
    prow = at("prow", H0, [88, P])
    vb_hl = at("vb_hl", R0, [P, NTOK, B_H, 2, HD], F32R)
    va_hl = at("va_hl", R0 + 32 * KB, [P, NTOK, A_KV, 2, HD], F32R)
    q_hl = [at(f"q_{s}", R0 + (40 + 8 * i) * KB, [P, 2, S], F32R) for i, s in enumerate(("hi", "lo"))]
    k_hl = [at(f"k_{s}", R0 + (56 + 8 * i) * KB, [P, 2, S], F32R) for i, s in enumerate(("hi", "lo"))]
    s_sb = at("s_sb", R0 + 72 * KB, [P, 2, S])
    pt_hl = [at(f"pt_{s}", R0 + (80 + 8 * i) * KB, [P, 4, NT], F32R) for i, s in enumerate(("hi", "lo"))]
    rope_a = at("rope_a", R0 + 96 * KB, [P, NT])
    rope_b = at("rope_b", R0 + 98 * KB, [P, NT])
    ostage = at("ostage", R0 + 100 * KB, [P, 4, P])
    o_sb = at("o_sb", R0 + 102 * KB, [P, 2, P])
    fg = [at(f"fg{i}", R0 + 103 * KB + 256 * i, [P, NTOK, B_H]) for i in range(7)]
    absz, ez, onep, lnp, corr, nlf, pref = fg
    ncum = at("ncum", R0 + 106 * KB, [B_H, S])
    ob_hl = [at(f"ob_{s}", R0 + 32 * i * KB, [P, KD, S], F32R) for i, s in enumerate(("hi", "lo"))]
    merged = at("merged", R0 + 64 * KB, [P, KD, S])
    sg = at("sg", R0 + 96 * KB, [P, 4, NT])
    adaraw = at("adaraw", R0 + XIN + 24 * KB, [P, 2, KD, P])
    grow = at("grow", R0 + CS, [P, 2, D])
    woraw = at("woraw", R0 + CS + 8 * KB, [P, 2, D])
    xr = at("xr", R0 + 64 * KB, [P, 2, D])
    x1 = at("x1", R0 + 72 * KB, [P, 2, D])
    xn = at("xn", R0 + 80 * KB, [P, 4, D])
    htmp2 = at("htmp2", R0 + 96 * KB, [P, 2, NT])
    junk2 = at("junk2", R0 + 100 * KB, [P, D])
    diag = at("diag", R0 + 96 * KB, [P, 4, P])
    act_ff = at("act_ff", R0, [P, FT, S])
    sl = at("sl", R0 + XIN + 24 * KB, [P, 4, NT])
    w2raw = at("w2raw", R0 + 88 * KB, [P, 2, NT])
    w2_hl = [at(f"w2_{s}", R0 + (92 + 4 * i) * KB, [P, 2, NT], F32R) for i, s in enumerate(("hi", "lo"))]
    ah_hl = [at(f"ah_{s}", H0 + 8 * i * KB, [P, 2, S], F32R) for i, s in enumerate(("hi", "lo"))]
    y0 = at("y0", H0 + 16 * KB, [P, NTOK, NT])
    x1r = at("x1r", H0 + 32 * KB, [P, 4, D])
    fin = at("fin", H0 + 48 * KB, [P, 2, D])
    junk3 = at("junk3", H0 + 56 * KB, [P, D])

    PAIRS = 8
    NU = PAIRS * NTOK * 2

    def parts(u):
        return u // 16, (u % 16) // 2, u % 2

    def width(u):
        p, i, _ = parts(u)
        return P * (min(i + 1, 2) if p < 4 else i + 1)

    def first_block(u):
        p, i, _ = parts(u)
        return max(i - 1, 0) if p < 4 else 0

    def v_of(u, blk, lo):
        p, _, h = parts(u)
        v = va_hl[:, blk, h] if p < 4 else vb_hl[:, blk, 2 * (p - 4) + h]
        return v[:, 0] if lo else v.rearrange("p a d -> p (a d)")

    p_groups = {}
    o_group = {}
    group_kind = []
    np_groups = 0
    for u in range(NU + 2):
        if u % 2 == 1 and u >= 3:
            o_group[(u - 3) // 2] = len(group_kind)
            group_kind.append(("o", (u - 3) // 2))
        if u < NU:
            nb = width(u) // P
            p_groups[u] = []
            for b0 in range(0, nb, 4):
                p_groups[u].append((len(group_kind), np_groups, range(b0, min(b0 + 4, nb))))
                group_kind.append(("p", np_groups))
                np_groups += 1

    chunks = [(0, 0, k_hl, 1, "rope"), (0, 1, k_hl, 1, "rope"), (1, 0, q_hl, 0, "rope"), (1, 1, q_hl, 0, "rope")]
    mm_at = {u: [] for u in range(NU)}
    evac_at = {u: [] for u in range(NU)}
    q_chunk = {0: (2, 3)}
    for p in range(PAIRS - 1):
        if p < 3:
            q_chunk[p + 1] = (len(chunks), len(chunks) + 1)
            for ch in range(CH):
                for s in range(6):
                    mm_at[16 * p + 8 * ch + s].append((len(chunks), 4 * s, 4 * s + 4))
                evac_at[16 * p + 8 * ch + 5].append(len(chunks))
                chunks.append((p + 2, ch, q_hl, (p + 1) % 2, "rope"))
        else:
            q_chunk[p + 1] = (len(chunks) + 2, len(chunks) + 3)
            for j in range(4):
                for s in range(3):
                    mm_at[16 * p + 4 * j + s].append((len(chunks), 8 * s, 8 * s + 8))
                evac_at[16 * p + 4 * j + 2].append(len(chunks))
                chunks.append((5 + 2 * (p - 3) + j // 2, j % 2, (k_hl, q_hl)[j // 2], (p + 1) % 2, "plain"))
    N_ROPE = 10
    N_ATT = 13
    N_BR = 3 * KD
    N_FF = N_ATT + N_BR
    N_ADA = 4 * KD

    def h_bank(g):
        return g % 4 if g < 2 * KD else 2 + g % 2

    def y_bank(t):
        return (0, 2, 4, 6, 0, 4, 6, 0)[t]

    with ExitStack() as ctx:
        PS = ctx.enter_context(nc.psum_tensor("PS", [P, 8, NT], F32))

        def sem(name):
            return ctx.enter_context(nc.semaphore(name))

        par_in, bc_in = sem("par_in"), sem("bc_in")
        x_in = [sem("x_in0"), sem("x_in1")]
        ada_in = [sem("ada_in0"), sem("ada_in1")]
        ada2_in = [sem("ada2_in0"), sem("ada2_in1")]
        wv_in = [sem(f"wv_in{k}") for k in range(KD)]
        w_in_s = [sem("w_in_s0"), sem("w_in_s1")]
        cum_in = [sem("cum_in0"), sem("cum_in1")]
        const_ok = sem("const_ok")
        prow_ready, pcols_ok = sem("prow_ready"), sem("pcols_ok")
        ada_used, ada_taken = sem("ada_used"), sem("ada_taken")
        xt_ready, h_hi, h_tmp, h_lo = sem("xt_ready"), sem("h_hi"), sem("h_tmp"), sem("h_lo")
        ssq_ok, var_ok, rms_ok, xn_ok = sem("ssq_ok"), sem("var_ok"), sem("rms_ok"), sem("xn_ok")
        reduced, tables = sem("reduced"), sem("tables")
        wv_hi_ok, wv_split = sem("wv_hi_ok"), sem("wv_split")
        v_ready, v_hi_ok, v_taken = sem("v_ready"), sem("v_hi_ok"), sem("v_taken")
        absz_ok, ez_ok, onep_ok, lnp_ok, nlf_ok = sem("absz_ok"), sem("ez_ok"), sem("onep_ok"), sem("lnp_ok"), sem("nlf_ok")
        cum_ready, cum_taken, cum_out = sem("cum_ready"), sem("cum_taken"), sem("cum_out")
        w_hi_ok, w_split = sem("w_hi_ok"), sem("w_split")
        proj_ready, proj_hi, proj_taken = sem("proj_ready"), sem("proj_hi"), sem("proj_taken")
        rope_sum, rope_hi, rope_done = sem("rope_sum"), sem("rope_hi"), sem("rope_done")
        s_ready, s_taken, p_ready = sem("s_ready"), sem("s_taken"), sem("p_ready")
        grp_ready, grp_hi, grp_lo = sem("grp_ready"), sem("grp_hi"), sem("grp_lo")
        pv_done, o_taken = sem("pv_done"), sem("o_taken")
        o_out = [sem(f"o_out{i}") for i in range(4)]
        dve_step, pool_step, act_step = sem("dve_step"), sem("pool_step"), sem("act_step")
        ob_in, ob_hi_ok, ob_split = sem("ob_in"), sem("ob_hi_ok"), sem("ob_split")
        g_ready, g_done = sem("g_ready"), sem("g_done")
        br_ready, br_taken, merged_ok = sem("br_ready"), sem("br_taken"), sem("merged_ok")
        wo_in = [sem("wo_in0"), sem("wo_in1")]
        wo_hi_ok, wo_split, m_hi_ok, m_split = sem("wo_hi_ok"), sem("wo_split"), sem("m_hi_ok"), sem("m_split")
        gcol_ok, diag_ok, grow_ready, grow_ok = sem("gcol_ok"), sem("diag_ok"), sem("grow_ready"), sem("grow_ok")
        xr_in = [sem("xr_in0"), sem("xr_in1")]
        x1_out = [sem("x1_out0"), sem("x1_out1")]
        y_ready, y_sq, y_var, y_rms = sem("y_ready"), sem("y_sq"), sem("y_var"), sem("y_rms")
        y_taken, x1_ok, x1_sq, x1_var, x1_rms, x1_rstd = (sem("y_taken"), sem("x1_ok"), sem("x1_sq"), sem("x1_var"),
                                                          sem("x1_rms"), sem("x1_rstd"))
        ff_ready, silu_ok, ff_ok = sem("ff_ready"), sem("silu_ok"), sem("ff_ok")
        w2_in = [sem("w2_in0"), sem("w2_in1")]
        w2_hi_ok, w2_split = sem("w2_hi_ok"), sem("w2_split")
        ah_hi_ok, ah_split, ah_used = sem("ah_hi_ok"), sem("ah_split"), sem("ah_used")
        z_ready, z_taken, z_sq, z_var, z_rms, fin_ok = (sem("z_ready"), sem("z_taken"), sem("z_sq"), sem("z_var"),
                                                        sem("z_rms"), sem("fin_ok"))
        x1r_in = [sem(f"x1r_in{i}") for i in range(4)]
        done = [sem("done0"), sem("done1")]

        block = ctx.enter_context(nc.Block())

        w_in_v = w_in[0].rearrange("(k p) n -> p k n", p=P)
        w_ada_v = w_ada[0].rearrange("(k p) n -> p k n", p=P)
        w_out_v = w_out[0].rearrange("(k p) n -> k p n", p=P)
        w_a_v = w_branch_a[0].rearrange("(f g d) n -> f d g n", f=2, d=HD)
        w_b_v = w_branch_b[0].rearrange("(k p) n -> p k n", p=P)
        w_fi_v = w_ffn_in[0].rearrange("(k p) n -> p k n", p=P)
        w_fo_v = w_ffn_out[0].rearrange("(k p) n -> p k n", p=P)
        x_v = x[0].rearrange("(t p) d -> t p d", p=P)
        out_v = out[0].rearrange("(t p) d -> t p d", p=P)

        UNIT = 48

        @block.sync
        def _(sp):
            at_row = 0
            for src in (c, b_ada, g_pre_mix, g_post_mix, g_pre_ffn, g_post_ffn):
                n = src.shape[1] // P
                sp.dma_start(prow[at_row:at_row + n, :], src[0].rearrange("(r p) -> r p", p=P)).then_inc(par_in, 16)
                at_row += n
            sp.dma_start(bfb[:, :], b_f[0].partition_broadcast(P)).then_inc(bc_in, 16)
            sp.dma_start(sinkb[:, :], sinks[0].partition_broadcast(P)).then_inc(bc_in, 16)
            sp.dma_start(posi[:, :], positions[0].partition_broadcast(P)).then_inc(bc_in, 16)
            sp.dma_start(invf[:, :], inv_freq).then_inc(bc_in, 16)
            for t in range(4):
                sp.dma_start(xin[:, t, :], x_v[t]).then_inc(x_in[0], 16)
            for k in range(KD):
                sp.dma_start(wvraw[:, k, 0:VB_W + B_H], w_in_v[:, k, C_VB:C_VB + VB_W + B_H]).then_inc(wv_in[k], 16)
                sp.dma_start(wvraw[:, k, VB_W + B_H:WV], w_in_v[:, k, C_VA:C_VA + VA_W]).then_inc(wv_in[k], 16)
            for j in range(4):
                if j >= 2:
                    sp.wait_ge(ada_used, j - 1)
                sp.dma_start(wada[:, j % 2], w_ada_v[:, :, j * NT:(j + 1) * NT]).then_inc(ada_in[j % 2], 16)
            for t in range(4, 8):
                sp.dma_start(xin[:, t, :], x_v[t]).then_inc(x_in[1], 16)

            sp.wait_ge(wv_split, KD)
            for n in range(N_ATT):
                if n >= 2:
                    sp.wait_ge(w_split, n - 1)
                if n == 0:
                    sp.dma_start(wraw[:, 0], w_in_v[:, :, C_KA:C_KA + P]).then_inc(w_in_s[0], UNIT)
                elif n < 5:
                    for f, col in enumerate((C_QA + (n - 1) * HD, C_QA + (n + 3) * HD)):
                        sp.dma_start(wraw[:, n % 2, :, f * HD:(f + 1) * HD],
                                     w_in_v[:, :, col:col + HD]).then_inc(w_in_s[n % 2], 16 + 16 * f)
                else:
                    col = (C_KB, C_QB)[(n - 5) % 2] + (n - 5) // 2 * P
                    sp.dma_start(wraw[:, n % 2], w_in_v[:, :, col:col + P]).then_inc(w_in_s[n % 2], UNIT)
                if n > 5 and n % 2 == 0:
                    p = 4 + (n - 5) // 2
                    slot = 1 - p % 2
                    if p == 4:
                        sp.wait_ge(cum_taken, CH)
                        sp.dma_start(ncum_dram, ncum[:, :]).then_inc(cum_out, 16)
                        sp.wait_ge(cum_out, 16)
                        sp.wait_ge(h_lo, 2 * KD)
                    elif p == 5:
                        sp.wait_ge(proj_taken, N_ROPE)
                    else:
                        sp.wait_ge(s_taken, 16 * (p - 1))
                    sp.dma_start(cs[:, slot], ncum_dram[2 * (p - 4):2 * (p - 4) + 2, :].partition_broadcast(P))\
                        .then_inc(cum_in[slot], 16)

            with sp.Fori(1, KD // 2 + 1) as it:
                for mm in range(2):
                    col = it * (2 * P) + (mm - 2) * P
                    for j in range(3):
                        n = N_ATT + 3 * mm + j
                        src = w_in_v[:, :, bass.ds(col + (C_G + j * D), P)] if j < 2 else None
                        sp.wait_ge(w_split, it * 6 + (n - 1 - 6))
                        if j < 2:
                            sp.dma_start(wraw[:, n % 2], src)\
                                .then_inc(w_in_s[n % 2], UNIT)
                        else:
                            for f in range(2):
                                sp.dma_start(wraw[f * HD:(f + 1) * HD, n % 2, 0:4, :], w_a_v[f, :, :, bass.ds(col, P)])\
                                    .then_inc(w_in_s[n % 2], 16)
                            sp.dma_start(wraw[:, n % 2, 4:8, :], w_b_v[:, :, bass.ds(col, P)]).then_inc(w_in_s[n % 2], 16)
                        for q in ((0,), (1,), (2, 3))[j]:
                            a = 4 * mm + q
                            sp.wait_ge(ada_used, it * 8 + (a + 3 - 8))
                            sp.dma_start(adaraw[:, a % 2], w_ada_v[:, :, bass.ds(it * (8 * P) + (16 * P + (a - 8) * P), P)])\
                                .then_inc(ada2_in[a % 2], 16)

            for k in range(KD):
                if k >= 2:
                    sp.wait_ge(wo_split, k - 1)
                sp.dma_start(woraw[:, k % 2], w_out_v[k]).then_inc(wo_in[k % 2], 16)
            for n in (N_FF, N_FF + 1):
                sp.wait_ge(w_split, n - 1)
                col = (n - N_FF) * DFF
                sp.dma_start(wraw[:, n % 2], w_fi_v[:, :, col:col + P]).then_inc(w_in_s[n % 2], UNIT)
            sp.wait_ge(m_split, 2 * KD)
            for t in range(2):
                sp.dma_start(xr[:, t], x_v[t]).then_inc(xr_in[t], 16)
            for t in range(NTOK):
                sp.wait_ge(x1_ok, t + 1)
                sp.dma_start(x1_dram[t], x1[:, t % 2]).then_inc(x1_out[t % 2], 16)
                if t + 2 < NTOK:
                    sp.dma_start(xr[:, t % 2], x_v[t + 2]).then_inc(xr_in[t % 2], 16)

            with sp.Fori(0, FT - 1) as it:
                for j in range(2):
                    n = N_FF + 2 + j
                    sp.wait_ge(w_split, it * 2 + (n - 1))
                    sp.dma_start(wraw[:, n % 2], w_fi_v[:, :, bass.ds(it * P + (P + j * DFF), P)])\
                        .then_inc(w_in_s[n % 2], UNIT)
            sp.wait_ge(xn_ok, 2 + NTOK)
            for half in range(2):
                with sp.Fori(0, FT // 2) as it:
                    for j in range(2):
                        sp.wait_ge(w2_split, it * 2 + (FT * half + j + 1))
                        sp.dma_start(w2raw[:, j], w_fo_v[:, bass.ds(it * 2 + j, 1), half * NT:(half + 1) * NT]
                                     .rearrange("p a n -> p (a n)")).then_inc(w2_in[j], 16)
                if half == 0:
                    sp.wait_ge(ff_ready, 4 * FT)
                    for i in range(2):
                        sp.wait_ge(x1_out[i], 16 * (NTOK // 2))
                    for t in range(4):
                        sp.dma_start(x1r[:, t], x1_dram[t]).then_inc(x1r_in[t], 16)
            for t in range(NTOK):
                sp.wait_ge(fin_ok, t + 1)
                sp.dma_start(out_v[t], fin[:, t % 2]).then_inc(done[t % 2], 16)
                if t + 4 < NTOK:
                    sp.dma_start(x1r[:, t % 4], x1_dram[t + 4]).then_inc(x1r_in[t % 4], 16)
            for i in range(2):
                sp.wait_ge(done[i], 16 * (NTOK // 2))

        @block.gpsimd
        def _(pool):
            step = [0]

            def link(ins):
                step[0] += 1
                ins.then_inc(pool_step, 1)
                pool.wait_ge(pool_step, step[0])

            link(pool.memset(ident[:, :], 0.0))
            link(pool.memset(ones[:, :], 1.0))
            link(pool.memset(band[:, :], 0.0))
            link(pool.affine_select(out=ident[:, :], in_=ident[:, :], compare_op=ALU.not_equal, fill=1.0,
                                    base=0, pattern=[[-1, P]], channel_multiplier=1))
            link(pool.affine_select(out=tri[:, :], in_=ones[:, :], compare_op=ALU.is_ge, fill=0.0,
                                    base=0, pattern=[[1, P]], channel_multiplier=-1))
            link(pool.affine_select(out=band[:, 0:P], in_=band[:, 0:P], compare_op=ALU.is_gt, fill=MASKED,
                                    base=0, pattern=[[1, P]], channel_multiplier=-1))
            link(pool.affine_select(out=band[:, P:2 * P], in_=band[:, P:2 * P], compare_op=ALU.is_ge, fill=MASKED,
                                    base=0, pattern=[[-1, P]], channel_multiplier=1))
            link(pool.tensor_copy(identb[:, :], ident[:, :]))
            link(pool.tensor_copy(causalb[:, :], band[:, P:2 * P]))
            for q in range(4):
                link(pool.memset(sgn[32 * q:32 * q + 32, :], 1.0 - 2.0 * (q % 2)))
            pool.memset(scratch[:, :], 0.0).then_inc(const_ok, 1)

            for k in range(KD):
                pool.wait_ge(wv_in[k], 32)
                pool.tensor_copy(wv_hl[0][:, k], wvraw[:, k]).then_inc(wv_hi_ok, 1)
                pool.wait_ge(wv_hi_ok, k + 1)
                pool.tensor_tensor(wv_hl[1][:, k], wvraw[:, k], wv_hl[0][:, k].bitcast(F32), ALU.subtract)\
                    .then_inc(wv_split, 1)

            def take_wait():
                pool.tensor_tensor(scratch[:, :], ones[:, 0:1], ones[:, 0:1], ALU.mult)

            def split_unit(slot, loads, n, att=False):
                pool.wait_ge(w_in_s[slot], loads)
                if not att:
                    take_wait()
                pool.tensor_copy(w_hl[0][:, slot], wraw[:, slot]).then_inc(w_hi_ok, 1)
                pool.wait_ge(w_hi_ok, n + 1)
                pool.tensor_tensor(w_hl[1][:, slot], wraw[:, slot], w_hl[0][:, slot].bitcast(F32), ALU.subtract)\
                    .then_inc(w_split, 1)

            def split_att(n):
                if n >= 2:
                    pool.wait_ge(proj_ready, 2 * (n - 1))
                split_unit(n % 2, UNIT * (n // 2 + 1), n, att=True)

            def rope_chunk(j):
                n, ch, dst, slot, _ = chunks[j]
                cols = slice(ch * NT, (ch + 1) * NT)
                pool.wait_ge(proj_taken, j + 1)
                pool.tensor_tensor(rope_a[:, :], rope_a[:, :], rope_b[:, :], ALU.add).then_inc(rope_sum, 1)
                pool.wait_ge(rope_sum, j + 1)
                if j >= 4:
                    pool.wait_ge(s_ready, 16 * (n - 2))
                pool.tensor_copy(dst[0][:, slot, cols], rope_a[:, :]).then_inc(rope_hi, 1)
                pool.wait_ge(rope_hi, j + 1)
                pool.tensor_tensor(dst[1][:, slot, cols], rope_a[:, :], dst[0][:, slot, cols].bitcast(F32),
                                   ALU.subtract).then_inc(rope_done, 1)

            split_att(0)
            split_att(1)
            for j in range(N_ROPE):
                rope_chunk(j)
                if j % 2 == 1:
                    split_att(chunks[j][0] + 2)
            for n in range(7, N_ATT):
                split_att(n)
            pool.wait_ge(proj_ready, len(chunks))
            with pool.Fori(0, KD // 2) as it:
                for mm in range(2):
                    for r in range(3):
                        n = N_ATT + 3 * mm + r
                        if r == 0:
                            pool.wait_ge(g_ready, it * 8 + (4 * mm + 4))
                        elif r == 1:
                            pool.wait_ge(br_ready, it * 8 + (4 * mm + 4))
                        else:
                            pool.wait_ge(g_ready, it * 8 + (4 * mm + 6))
                        split_unit(n % 2, it * (3 * UNIT) + UNIT * (n // 2 + 1), it * 6 + n)
            for n, last_use in ((N_FF, g_ready), (N_FF + 1, br_ready)):
                pool.wait_ge(last_use, 4 + 4 * KD)
                split_unit(n % 2, UNIT * (n // 2 + 1), n)
            for t in range(NTOK):
                if t >= 4:
                    pool.wait_ge(xt_ready, 3 * KD)
                pool.wait_ge(x1_rstd, t + 1)
                pool.tensor_scalar(xn[:, t % 4], x1[:, t % 2], rstd[:, 16 + t:17 + t], None, ALU.mult).then_inc(xn_ok, 1)
            with pool.Fori(0, FT - 1) as it:
                for j in range(2):
                    n = N_FF + 2 + j
                    pool.wait_ge(ff_ready, it * 4 + (2 * j + 2))
                    split_unit(n % 2, it * UNIT + UNIT * (n // 2 + 1), it * 2 + n)
            for half in range(2):
                with pool.Fori(0, FT // 2) as it:
                    for j in range(2):
                        i0 = FT * half + j
                        pool.wait_ge(w2_in[j], it * 16 + 16 * (FT // 2 * half + 1))
                        pool.wait_ge(ah_used, it * 2 + (i0 + 1))
                        take_wait()
                        pool.tensor_copy(w2_hl[0][:, j], w2raw[:, j]).then_inc(w2_hi_ok, 1)
                        pool.wait_ge(w2_hi_ok, it * 2 + (i0 + 1))
                        pool.tensor_tensor(w2_hl[1][:, j], w2raw[:, j], w2_hl[0][:, j].bitcast(F32), ALU.subtract)\
                            .then_inc(w2_split, 1)

        @block.scalar
        def _(act):
            def norm_rows(half):
                act.wait_ge(x_in[half], 64)
                for t in range(4 * half, 4 * half + 4):
                    nc.scalar.activation(junk[:, :], xin[:, t], ACT.Square, accum_out=ssq[:, t:t + 1]).then_inc(ssq_ok, 1)
                    act.wait_ge(ssq_ok, t + 1)
                act.wait_ge(var_ok, half + 1)
                nc.scalar.activation(rms[:, 4 * half:4 * half + 4], var[:, 4 * half:4 * half + 4], ACT.Sqrt)\
                    .then_inc(rms_ok, 1)

            def h_hi_part(g, scale, shift):
                act.wait_ge(xt_ready, g + 1)
                k, half = g % KD, g // KD % 2
                nc.scalar.activation(act_hl[0][:, k, half * NT:(half + 1) * NT], PS[:, h_bank(g)], ACT.Identity,
                                     bias=shift[:, k:k + 1], scale=scale[:, k:k + 1]).then_inc(h_hi, 1)

            def v_hi_part(t):
                act.wait_ge(v_ready, 2 * t + 1)
                nc.scalar.activation(va_hl[:, t, :, 0, :], PS[:, 7, B_H:B_H + VA_W].rearrange("p (h d) -> p h d", h=A_KV),
                                     ACT.Copy).then_inc(v_hi_ok, 1)
                act.wait_ge(v_ready, 2 * t + 2)
                nc.scalar.activation(vb_hl[:, t, :, 0, :], PS[:, 5 + t % 2, 0:VB_W].rearrange("p (h d) -> p h d", h=B_H),
                                     ACT.Copy).then_inc(v_hi_ok, 1)

            norm_rows(0)
            act.wait_ge(const_ok, 1)
            act.wait_ge(reduced, 2)
            nc.scalar.activation(cs[:, 0, 0], cs[:, 0, 0], ACT.Sin).then_inc(tables, 1)
            nc.scalar.activation(cs[:, 0, 1], cs[:, 0, 1], ACT.Sin, scale=sgn[:, 0:1]).then_inc(tables, 1)
            act.wait_ge(ada_taken, 1)
            for g in range(KD):
                h_hi_part(g, a_mix, adac)
            norm_rows(1)
            v_hi_part(0)
            for t in range(2):
                for g in range(KD + 4 * t, KD + 4 * t + 4):
                    h_hi_part(g, a_mix, adac)
                v_hi_part(t + 1)
            for t in range(3, NTOK):
                v_hi_part(t)

            act.wait_ge(absz_ok, 1)
            nc.scalar.activation(ez[:, :, :], absz[:, :, :], ACT.Exp, scale=-1.0).then_inc(ez_ok, 1)
            act.wait_ge(onep_ok, 1)
            nc.scalar.activation(lnp[:, :, :], onep[:, :, :], ACT.Ln).then_inc(lnp_ok, 1)

            def exps(u):
                w = width(u) + (u < 64)
                act.wait_ge(s_taken, u + 1)
                if u >= 4:
                    act.wait_ge(o_taken, (u - 4) // 2 + 1)
                nc.scalar.activation(s_sb[:, u % 2, 0:w], s_sb[:, u % 2, 0:w], ACT.Exp, bias=nmax[:, u % 4:u % 4 + 1],
                                     scale=-1.0, accum_out=den[:, u % 4:u % 4 + 1]).then_inc(p_ready, 1)

            def group_hi(g, slot, n):
                act.wait_ge(grp_ready, g + 1)
                if slot >= 4:
                    act.wait_ge(pv_done, slot - 3)
                nc.scalar.activation(pt_hl[0][:, slot % 4, 0:n], PS[:, 5 + g % 2, 0:n], ACT.Copy).then_inc(grp_hi, 1)

            def out_tile(tile):
                g = o_group[tile]
                act.wait_ge(grp_ready, g + 1)
                if tile >= 4:
                    act.wait_ge(o_out[tile % 4], 16 * (tile // 4))
                nc.scalar.activation(ostage[:, tile % 4], PS[:, 5 + g % 2, 0:P], ACT.Copy).then_inc(grp_hi, 1)
                return g

            def send_tile(tile):
                act.wait_ge(grp_hi, o_group[tile] + 1)
                p, i = tile // NTOK, tile % NTOK
                act.dma_start(oT_dram[p, :, i * P:(i + 1) * P], ostage[:, tile % 4]).then_inc(o_out[tile % 4], 16)

            exps(0)
            for u in range(NU + 2):
                if u + 1 < NU:
                    exps(u + 1)
                if u % 2 == 1 and u >= 3:
                    out_tile((u - 3) // 2)
                if u < NU:
                    for g, slot, blocks in p_groups[u]:
                        group_hi(g, slot, P * len(blocks))
                if u % 2 == 1 and u >= 3:
                    send_tile((u - 3) // 2)
                for j in evac_at[u] if u < NU else ():
                    if chunks[j][4] == "plain":
                        _, ch, dst, slot, _ = chunks[j]
                        act.wait_ge(proj_ready, j + 1)
                        nc.scalar.activation(dst[0][:, slot, ch * NT:(ch + 1) * NT], PS[:, 0], ACT.Copy).then_inc(proj_hi, 1)

            act.wait_ge(pv_done, np_groups)
            for i in range(4):
                act.wait_ge(o_out[i], 16 * (PAIRS * NTOK // 4))
            for p in range(8):
                act.dma_start(merged[:, p, :], oT_dram[p]).then_inc(ob_in, 16)

            def gate(m4, m2, j):
                act.wait_ge(g_ready, m4 + (j + 5))
                act.wait_ge(merged_ok, m2 + (j % 2 + 1))
                nc.scalar.activation(sg[:, j], PS[:, j], ACT.Sigmoid).then_inc(g_done, 1)

            def outputs_hi(p):
                nc.scalar.activation(ob_hl[0][:, p], merged[:, p], ACT.Copy).then_inc(ob_hi_ok, 1)

            act.wait_ge(ob_in, 16 * 8)
            for p in range(8):
                outputs_hi(p)
            with act.Fori(0, KD // 2) as it:
                for mm in range(2):
                    for j in range(4):
                        gate(it * 8 + 4 * mm, it * 4 + 2 * mm, j)

            def merged_hi(k, half):
                cols = slice(half * NT, (half + 1) * NT)
                nc.scalar.activation(act_hl[0][:, k, cols], merged[:, k, cols], ACT.Copy).then_inc(m_hi_ok, 1)

            act.wait_ge(br_ready, 4 + 4 * KD)
            act.wait_ge(merged_ok, 2 + 2 * KD)
            for k in range(KD):
                act.wait_ge(wo_in[k % 2], 16 * (k // 2 + 1))
                nc.scalar.activation(ob_hl[0][:, k], woraw[:, k % 2], ACT.Copy).then_inc(wo_hi_ok, 1)
                merged_hi(k, 0)
            for k in range(KD):
                merged_hi(k, 1)
            for i in range(2):
                for hb in range(2):
                    act.wait_ge(grow_ready, 2 * i + hb + 1)
                    nc.scalar.activation(grow[:, i, hb * NT:(hb + 1) * NT], PS[:, 6 + hb], ACT.Copy).then_inc(grow_ok, 1)

            def y_squares(t):
                b = y_bank(t)
                act.wait_ge(y_ready, t + 1)
                if t > 0:
                    act.wait_ge(x1_sq, t)
                else:
                    act.wait_ge(m_split, 2 * KD)
                nc.scalar.activation(junk2[:, :], PS[:, b:b + 2].rearrange("p a n -> p (a n)"), ACT.Square,
                                     accum_out=ssq[:, 8 + t:9 + t]).then_inc(y_sq, 1)
                act.wait_ge(y_var, t + 1)
                nc.scalar.activation(rms[:, 8 + t:9 + t], var[:, 8 + t:9 + t], ACT.Sqrt).then_inc(y_rms, 1)

            def x1_squares(t):
                act.wait_ge(x1_ok, t + 1)
                nc.scalar.activation(junk2[:, :], x1[:, t % 2], ACT.Square, accum_out=ssq[:, 16 + t:17 + t])\
                    .then_inc(x1_sq, 1)
                act.wait_ge(x1_var, t + 1)
                nc.scalar.activation(rms[:, 16 + t:17 + t], var[:, 16 + t:17 + t], ACT.Sqrt).then_inc(x1_rms, 1)

            for t in range(NTOK):
                y_squares(t)
                x1_squares(t)
                if t in (4, 7):
                    for k in range(KD):
                        h_hi_part(KD * (2 + (t - 4) // 3) + k, a_ffn, adac[:, 3 * KD:4 * KD])

            with act.Fori(0, FT // 2) as it:
                for ff in range(2):
                    for ch in range(CH):
                        act.wait_ge(ff_ready, it * 8 + (4 * ff + ch + 1))
                        act.wait_ge(ff_ok, it * 4 + (2 * ff + ch + 1))
                        nc.scalar.activation(sl[:, 2 * ff + ch], PS[:, 4 * ff + ch], ACT.Silu).then_inc(silu_ok, 1)
            act.wait_ge(ff_ready, 4 * FT)
            act.wait_ge(ff_ok, 4 + 2 * FT)
            for half in range(2):
                with act.Fori(0, FT // 2) as it:
                    for j in range(2):
                        act.wait_ge(ah_used, it * 2 + (FT * half + j + 1))
                        nc.scalar.activation(ah_hl[0][:, j], act_ff[:, bass.ds(it * 2 + j, 1), :]
                                             .rearrange("p a n -> p (a n)"), ACT.Copy).then_inc(ah_hi_ok, 1)
                if half == 0:
                    for t in range(NTOK):
                        act.wait_ge(z_taken, t + 1)
                        if t > 0:
                            act.wait_ge(z_sq, t)
                        nc.scalar.activation(junk3[:, 0:NT], y0[:, t], ACT.Square, accum_out=ssq[:, 24 + t:25 + t])\
                            .then_inc(z_sq, 1)
            for t in range(NTOK):
                act.wait_ge(z_ready, NTOK + t + 1)
                act.wait_ge(z_sq, NTOK + t)
                nc.scalar.activation(junk3[:, 0:NT], PS[:, t], ACT.Square, accum_out=ssq_b[:, t:t + 1]).then_inc(z_sq, 1)
                act.wait_ge(z_var, t + 1)
                nc.scalar.activation(rms[:, 24 + t:25 + t], var[:, 24 + t:25 + t], ACT.Sqrt).then_inc(z_rms, 1)

        @block.vector
        def _(dve):
            step = [0]

            def link(ins):
                step[0] += 1
                ins.then_inc(dve_step, 1)
                dve.wait_ge(dve_step, step[0])

            nc.vector.memset(credit[:, 0:1], 0.0).then_inc(merged_ok, 2)
            nc.vector.memset(credit[:, 1:2], 0.0).then_inc(ff_ok, 4)
            nc.vector.memset(credit[:, 2:3], 0.0).then_inc(br_taken, 4)
            nc.vector.memset(credit[:, 3:4], 0.0).then_inc(ah_used, 2)
            nc.vector.memset(credit[:, 4:5], 0.0).then_inc(w2_split, 2)
            nc.vector.memset(credit[:, 5:6], 0.0).then_inc(g_ready, 4)
            nc.vector.memset(credit[:, 6:7], 0.0).then_inc(br_ready, 4)
            nc.vector.memset(credit[:, 7:8], 0.0).then_inc(g_done, 4)

            dve.wait_ge(bc_in, 64)
            link(nc.vector.tensor_copy(ang[:, :], posi[:, :]))
            link(nc.vector.tensor_scalar(ang[:, :], ang[:, :], invf[:, 0:1], None, ALU.mult))
            for which, quarter in ((0, 0.25), (1, 0.0)):
                r = cs[:, 0, which]
                link(nc.vector.tensor_scalar(turns[:, :], ang[:, :], 1.0 / (2 * math.pi), quarter, ALU.mult, ALU.add))
                link(nc.vector.tensor_scalar(turns[:, :], turns[:, :], ROUND, ROUND, ALU.add, ALU.subtract))
                link(nc.vector.scalar_tensor_tensor(out=r, in0=turns[:, :], scalar=-TURN[0], in1=ang[:, :],
                                                    op0=ALU.mult, op1=ALU.add))
                for part in TURN[1:]:
                    link(nc.vector.scalar_tensor_tensor(out=r, in0=turns[:, :], scalar=-part, in1=r,
                                                        op0=ALU.mult, op1=ALU.add))
                link(nc.vector.tensor_scalar(r, r, 2 * math.pi * quarter, PI_BELOW, ALU.add, ALU.min))
                nc.vector.tensor_scalar(r, r, -PI_BELOW, None, ALU.max).then_inc(reduced, 1)

            def norm_rows(half):
                cols = slice(4 * half, 4 * half + 4)
                dve.wait_ge(ssq_ok, 4 * half + 4)
                nc.vector.tensor_scalar(var[:, cols], ssq[:, cols], 1.0 / D, EPS, ALU.mult, ALU.add).then_inc(var_ok, 1)
                dve.wait_ge(rms_ok, half + 1)
                link(nc.vector.reciprocal(rstd[:, cols], rms[:, cols]))
                for t in range(4 * half, 4 * half + 4):
                    ins = nc.vector.tensor_scalar(xin[:, t], xin[:, t], rstd[:, t:t + 1], None, ALU.mult)
                ins.then_inc(xn_ok, 1)

            norm_rows(0)
            dve.wait_ge(bc_in, 64)
            link(nc.vector.tensor_scalar(nsink[:, :], sinkb[:, :], -1.0, None, ALU.mult))
            dve.wait_ge(prow_ready, 1)
            nc.vector.tensor_copy(pcols[:, :], PS[:, 5, 0:88]).then_inc(pcols_ok, 1)
            dve.wait_ge(pcols_ok, 1)
            dve.wait_ge(ada_used, 4)
            link(nc.vector.tensor_tensor(adac[:, 0:2 * KD], PS[:, 4, 0:2 * KD], pcols[:, KD:3 * KD], ALU.add))
            nc.vector.scalar_tensor_tensor(out=a_mix[:, :], in0=adac[:, KD:2 * KD], scalar=1.0,
                                           in1=pcols[:, 7 * KD:8 * KD], op0=ALU.add, op1=ALU.mult).then_inc(ada_taken, 1)
            dve.wait_ge(ada_taken, 1)

            def h_lo_part(g, scale, shift, tmp):
                k, half = g % KD, g // KD % 2
                dve.wait_ge(h_hi, g + 1)
                nc.vector.tensor_scalar(tmp[:, g % 2], PS[:, h_bank(g)], scale[:, k:k + 1], shift[:, k:k + 1],
                                        ALU.mult, ALU.add).then_inc(h_tmp, 1)
                dve.wait_ge(h_tmp, g + 1)
                cols = slice(half * NT, (half + 1) * NT)
                nc.vector.tensor_tensor(act_hl[1][:, k, cols], tmp[:, g % 2], act_hl[0][:, k, cols].bitcast(F32),
                                        ALU.subtract).then_inc(h_lo, 1)

            def v_lo_part(t):
                dve.wait_ge(v_hi_ok, 2 * t + 1)
                if t == 0:
                    dve.wait_ge(bc_in, 64)
                nc.vector.tensor_tensor(z[:, t], PS[:, 7, 0:B_H], bfb[:, :], ALU.add)
                nc.vector.tensor_tensor(va_hl[:, t, :, 1, :], PS[:, 7, B_H:B_H + VA_W].rearrange("p (h d) -> p h d", h=A_KV),
                                        va_hl[:, t, :, 0, :].bitcast(F32), ALU.subtract).then_inc(v_taken, 1)
                dve.wait_ge(v_hi_ok, 2 * t + 2)
                nc.vector.tensor_tensor(vb_hl[:, t, :, 1, :], PS[:, 5 + t % 2, 0:VB_W].rearrange("p (h d) -> p h d", h=B_H),
                                        vb_hl[:, t, :, 0, :].bitcast(F32), ALU.subtract).then_inc(v_taken, 1)

            for g in range(KD):
                h_lo_part(g, a_mix, adac, htmp)
            norm_rows(1)
            v_lo_part(0)
            for t in range(2):
                for g in range(KD + 4 * t, KD + 4 * t + 4):
                    h_lo_part(g, a_mix, adac, htmp)
                v_lo_part(t + 1)
            for t in range(3, NTOK):
                v_lo_part(t)

            dve.wait_ge(v_taken, 2 * NTOK)
            nc.vector.scalar_tensor_tensor(out=absz[:, :, :], in0=z[:, :, :], scalar=-1.0, in1=z[:, :, :],
                                           op0=ALU.mult, op1=ALU.max).then_inc(absz_ok, 1)
            dve.wait_ge(ez_ok, 1)
            nc.vector.tensor_scalar(onep[:, :, :], ez[:, :, :], 1.0, None, ALU.add).then_inc(onep_ok, 1)
            dve.wait_ge(onep_ok, 1)
            link(nc.vector.scalar_tensor_tensor(out=corr[:, :, :], in0=onep[:, :, :], scalar=-1.0, in1=ez[:, :, :],
                                                op0=ALU.add, op1=ALU.subtract))
            dve.wait_ge(lnp_ok, 1)
            link(nc.vector.tensor_tensor(lnp[:, :, :], lnp[:, :, :], corr[:, :, :], ALU.subtract))
            link(nc.vector.scalar_tensor_tensor(out=nlf[:, :, :], in0=z[:, :, :], scalar=0.0, in1=lnp[:, :, :],
                                                op0=ALU.min, op1=ALU.subtract))
            link(nc.vector.tensor_scalar(nlf[:, :, :], nlf[:, :, :], -1.0, None, ALU.mult))
            link(nc.vector.memset(pref[:, 0], 0.0))
            for t in range(1, NTOK):
                ins = nc.vector.tensor_tensor(pref[:, t], pref[:, t - 1], nlf[:, t - 1], ALU.add)
                if t < NTOK - 1:
                    link(ins)
                else:
                    ins.then_inc(nlf_ok, 1)
            for cc in range(CH):
                dve.wait_ge(cum_ready, cc + 1)
                nc.vector.tensor_scalar(ncum[:, cc * NT:(cc + 1) * NT], PS[0:B_H, 5 + cc, :], 1.0 / SM, None, ALU.mult)\
                    .then_inc(cum_taken, 1)

            def rope_products(j, bank):
                ch = chunks[j][1]
                cols = slice(ch * NT, (ch + 1) * NT)
                dve.wait_ge(proj_ready, j + 1)
                if j == 0:
                    dve.wait_ge(tables, 2)
                else:
                    dve.wait_ge(rope_done, j)
                nc.vector.tensor_tensor(rope_a[:, :], PS[:, bank], cs[:, 0, 0, cols], ALU.mult)
                for quad in range(4):
                    o, i = 32 * quad, 32 * (quad ^ 1)
                    ins = nc.vector.tensor_tensor(rope_b[o:o + 32, :], PS[i:i + 32, bank], cs[i:i + 32, 0, 1, cols], ALU.mult)
                ins.then_inc(proj_taken, 1)

            for j in range(4):
                rope_products(j, j)

            def max_and_scale(u):
                p, i, h = parts(u)
                w = width(u)
                dve.wait_ge(s_ready, u + 1)
                if u >= 2:
                    dve.wait_ge(grp_ready, p_groups[u - 2][-1][0] + 1)
                src = PS[:, 1 + 2 * (u % 2):3 + 2 * (u % 2)].rearrange("p a n -> p (a n)")[:, 0:w]
                if p < 4:
                    sink = nsink[:, p + 4 * h:p + 4 * h + 1]
                    bias, least = band[:, 2 * P - w:2 * P], sink
                    nc.vector.tensor_copy(s_sb[:, u % 2, w:w + 1], sink)
                else:
                    slot = 1 - p % 2
                    if i == 0 and h == 0:
                        dve.wait_ge(cum_in[slot], 16 * ((p - 4) // 2 + 1))
                    bias, least = cs[:, slot, h, 0:w], BIG
                nc.vector.tensor_tensor_reduce(out=s_sb[:, u % 2, 0:w], in0=src, in1=bias, scale=-SM, scalar=least,
                                               op0=ALU.add, op1=ALU.min, accum_out=nmax[:, u % 4:u % 4 + 1])\
                    .then_inc(s_taken, 1)

            def group_lo(g, slot, n):
                dve.wait_ge(grp_hi, g + 1)
                nc.vector.tensor_tensor(pt_hl[1][:, slot % 4, 0:n], PS[:, 5 + g % 2, 0:n],
                                        pt_hl[0][:, slot % 4, 0:n].bitcast(F32), ALU.subtract).then_inc(grp_lo, 1)

            def normalise(tile):
                u = 2 * tile
                link(nc.vector.reciprocal(rden[:, :], den[:, u % 4:u % 4 + 2]))
                dve.wait_ge(pv_done, p_groups[u + 1][-1][1] + 1)
                for h in range(2):
                    link(nc.vector.tensor_scalar(ot[:, h], PS[:, 7, h * P + HALF:(h + 1) * P], rden[:, h:h + 1], None, ALU.mult))
                if tile >= 2:
                    dve.wait_ge(grp_ready, o_group[tile - 2] + 1)
                for h in range(2):
                    ins = nc.vector.scalar_tensor_tensor(out=o_sb[:, tile % 2, h * HALF:(h + 1) * HALF],
                                                         in0=PS[:, 7, h * P:h * P + HALF], scalar=rden[:, h:h + 1],
                                                         in1=ot[:, h], op0=ALU.mult, op1=ALU.add)
                ins.then_inc(o_taken, 1)

            max_and_scale(0)
            for u in range(NU + 1):
                if u + 1 < NU:
                    max_and_scale(u + 1)
                if u < NU:
                    for g, slot, blocks in p_groups[u]:
                        group_lo(g, slot, P * len(blocks))
                for j in evac_at[u] if u < NU else ():
                    _, ch, dst, slot, kind = chunks[j]
                    cols = slice(ch * NT, (ch + 1) * NT)
                    if kind == "rope":
                        rope_products(j, 0)
                    else:
                        dve.wait_ge(proj_hi, j - N_ROPE + 1)
                        nc.vector.tensor_tensor(dst[1][:, slot, cols], PS[:, 0], dst[0][:, slot, cols].bitcast(F32),
                                                ALU.subtract).then_inc(proj_taken, 1)
                if u >= 2 and u % 2 == 0:
                    normalise((u - 2) // 2)

            for p in range(8):
                dve.wait_ge(ob_hi_ok, p + 1)
                nc.vector.tensor_tensor(ob_hl[1][:, p], merged[:, p], ob_hl[0][:, p].bitcast(F32), ALU.subtract)\
                    .then_inc(ob_split, 1)
            with dve.Fori(0, KD // 2) as it:
                for mm in range(2):
                    for j in range(4):
                        dve.wait_ge(g_done, it * 8 + (4 * mm + j + 5))
                        dve.wait_ge(br_ready, it * 8 + (4 * mm + j + 5))
                        nc.vector.tensor_tensor(sg[:, j], PS[:, BR_BANK[j]], sg[:, j], ALU.mult).then_inc(br_taken, 1)
                    for ch in range(CH):
                        dve.wait_ge(br_taken, it * 8 + (4 * mm + ch + 7))
                        nc.vector.tensor_tensor(merged[:, bass.ds(it * 2 + mm, 1), ch * NT:(ch + 1) * NT]
                                                .rearrange("p a n -> p (a n)"), sg[:, ch], sg[:, 2 + ch], ALU.add)\
                            .then_inc(merged_ok, 1)

            def merged_lo(k, half):
                cols = slice(half * NT, (half + 1) * NT)
                dve.wait_ge(m_hi_ok, half * KD + k + 1)
                nc.vector.tensor_tensor(act_hl[1][:, k, cols], merged[:, k, cols], act_hl[0][:, k, cols].bitcast(F32),
                                        ALU.subtract).then_inc(m_split, 1)

            dve.wait_ge(merged_ok, 2 + 2 * KD)
            for k in range(KD):
                dve.wait_ge(wo_hi_ok, k + 1)
                nc.vector.tensor_tensor(ob_hl[1][:, k], woraw[:, k % 2], ob_hl[0][:, k].bitcast(F32), ALU.subtract)\
                    .then_inc(wo_split, 1)
                merged_lo(k, 0)
            dve.wait_ge(ada_used, 4 + N_ADA)
            link(nc.vector.tensor_tensor(adac[:, 2 * KD:6 * KD], PS[:, 7, 0:N_ADA], pcols[:, 3 * KD:7 * KD], ALU.add))
            nc.vector.tensor_tensor(gm_col[:, 0:KD], adac[:, 2 * KD:3 * KD], pcols[:, 8 * KD:9 * KD], ALU.mult)
            nc.vector.tensor_tensor(gm_col[:, KD:2 * KD], adac[:, 5 * KD:6 * KD], pcols[:, 10 * KD:11 * KD], ALU.mult)
            link(nc.vector.scalar_tensor_tensor(out=a_ffn[:, :], in0=adac[:, 4 * KD:5 * KD], scalar=1.0,
                                                in1=pcols[:, 9 * KD:10 * KD], op0=ALU.add, op1=ALU.mult))
            for r in range(4):
                if r > 0:
                    dve.wait_ge(grow_ready, r)
                for kk in range(4):
                    ins = nc.vector.tensor_scalar(diag[:, kk], ident[:, :], gm_col[:, 4 * r + kk:4 * r + kk + 1], None, ALU.mult)
                ins.then_inc(diag_ok, 1)
            for k in range(KD):
                merged_lo(k, 1)

            def residual(t):
                b = y_bank(t)
                dve.wait_ge(y_sq, t + 1)
                nc.vector.tensor_scalar(var[:, 8 + t:9 + t], ssq[:, 8 + t:9 + t], 1.0 / D, EPS, ALU.mult, ALU.add).then_inc(y_var, 1)
                dve.wait_ge(y_rms, t + 1)
                link(nc.vector.reciprocal(rstd[:, 8 + t:9 + t], rms[:, 8 + t:9 + t]))
                if t == 0:
                    dve.wait_ge(grow_ok, 4)
                if t >= 2:
                    dve.wait_ge(x1_out[t % 2], 16 * (t // 2))
                    dve.wait_ge(xn_ok, 2 + t - 1)
                nc.vector.scalar_tensor_tensor(out=x1[:, t % 2], in0=PS[:, b:b + 2].rearrange("p a n -> p (a n)"),
                                               scalar=rstd[:, 8 + t:9 + t], in1=grow[:, 0], op0=ALU.mult,
                                               op1=ALU.mult).then_inc(y_taken, 1)
                dve.wait_ge(y_taken, t + 1)
                dve.wait_ge(xr_in[t % 2], 16 * (t // 2 + 1))
                nc.vector.tensor_tensor(x1[:, t % 2], x1[:, t % 2], xr[:, t % 2], ALU.add).then_inc(x1_ok, 1)
                dve.wait_ge(x1_sq, t + 1)
                nc.vector.tensor_scalar(var[:, 16 + t:17 + t], ssq[:, 16 + t:17 + t], 1.0 / D, EPS, ALU.mult, ALU.add).then_inc(x1_var, 1)
                dve.wait_ge(x1_rms, t + 1)
                nc.vector.reciprocal(rstd[:, 16 + t:17 + t], rms[:, 16 + t:17 + t]).then_inc(x1_rstd, 1)

            for t in range(NTOK):
                residual(t)
                if t in (4, 7):
                    for k in range(KD):
                        h_lo_part(KD * (2 + (t - 4) // 3) + k, a_ffn, adac[:, 3 * KD:4 * KD], htmp2)

            with dve.Fori(0, FT // 2) as it:
                for ff in range(2):
                    for ch in range(CH):
                        dve.wait_ge(silu_ok, it * 4 + (2 * ff + ch + 1))
                        dve.wait_ge(ff_ready, it * 8 + (4 * ff + 2 + ch + 1))
                        nc.vector.tensor_tensor(act_ff[:, bass.ds(it * 2 + ff, 1), ch * NT:(ch + 1) * NT]
                                                .rearrange("p a n -> p (a n)"), PS[:, 4 * ff + 2 + ch], sl[:, 2 * ff + ch],
                                                ALU.mult).then_inc(ff_ok, 1)
            for half in range(2):
                with dve.Fori(0, FT // 2) as it:
                    for j in range(2):
                        dve.wait_ge(ah_hi_ok, it * 2 + (FT * half + j + 1))
                        nc.vector.tensor_tensor(ah_hl[1][:, j], act_ff[:, bass.ds(it * 2 + j, 1), :]
                                                .rearrange("p a n -> p (a n)"), ah_hl[0][:, j].bitcast(F32),
                                                ALU.subtract).then_inc(ah_split, 1)
                if half == 0:
                    for t in range(NTOK):
                        dve.wait_ge(z_ready, t + 1)
                        nc.vector.tensor_copy(y0[:, t], PS[:, t]).then_inc(z_taken, 1)
            for t in range(NTOK):
                dve.wait_ge(z_sq, NTOK + t + 1)
                link(nc.vector.tensor_tensor(ssq[:, 24 + t:25 + t], ssq[:, 24 + t:25 + t], ssq_b[:, t:t + 1], ALU.add))
                nc.vector.tensor_scalar(var[:, 24 + t:25 + t], ssq[:, 24 + t:25 + t], 1.0 / D, EPS, ALU.mult, ALU.add).then_inc(z_var, 1)
                dve.wait_ge(z_rms, t + 1)
                link(nc.vector.reciprocal(rstd[:, 24 + t:25 + t], rms[:, 24 + t:25 + t]))
                if t >= 2:
                    dve.wait_ge(done[t % 2], 16 * (t // 2))
                dve.wait_ge(x1r_in[t % 4], 16 * (t // 4 + 1))
                for hb, y in ((0, y0[:, t]), (1, PS[:, t])):
                    ins = nc.vector.scalar_tensor_tensor(out=fin[:, t % 2, hb * NT:(hb + 1) * NT], in0=y,
                                                         scalar=rstd[:, 24 + t:25 + t],
                                                         in1=grow[:, 1, hb * NT:(hb + 1) * NT], op0=ALU.mult, op1=ALU.mult)
                link(ins)
                nc.vector.tensor_tensor(fin[:, t % 2], fin[:, t % 2], x1r[:, t % 4], ALU.add).then_inc(fin_ok, 1)

        @block.tensor
        def _(pe):
            def product(out_ap, lhs, rhs, first, last):
                for i, (a, b) in enumerate(TERMS):
                    ins = nc.tensor.matmul(out_ap, lhs[a], rhs[b], start=first and i == 0, stop=last and i == 2)
                return ins

            def transpose_group(g, src):
                k = g % KD
                if 4 <= g < 2 * KD:
                    pe.wait_ge(h_tmp, g - 3)
                elif g >= 2 * KD + 2:
                    pe.wait_ge(h_tmp, g - 1)
                for tt in range(4):
                    ins = nc.tensor.transpose(PS[:, h_bank(g), tt * P:(tt + 1) * P], src[:, tt, k * P:(k + 1) * P], ident[:, :])
                ins.then_inc(xt_ready, 1)

            def ada_column(raw, column, sem_, n=1):
                for k in range(KD):
                    ins = nc.tensor.matmul(column, raw[:, k], pcols[:, k:k + 1], start=(k == 0), stop=(k == KD - 1))
                return ins

            pe.wait_ge(par_in, 96)
            pe.wait_ge(const_ok, 1)
            nc.tensor.transpose(PS[:, 5, 0:88], prow[:, :], ident[0:88, 0:88]).then_inc(prow_ready, 1)
            pe.wait_ge(xn_ok, 1)
            for g in range(4):
                transpose_group(g, xin[:, 0:4])
            pe.wait_ge(pcols_ok, 1)
            for j in range(4):
                pe.wait_ge(ada_in[j % 2], 16 * (j // 2 + 1))
                for oc in range(4):
                    for k in range(KD):
                        ins = nc.tensor.matmul(PS[:, 4, 4 * j + oc:4 * j + oc + 1], wada[:, j % 2, k, oc * P:(oc + 1) * P],
                                               pcols[:, k:k + 1], start=(k == 0), stop=(k == KD - 1))
                ins.then_inc(ada_used, 1)
            for g in range(4, KD):
                transpose_group(g, xin[:, 0:4])

            def values(t):
                cols = slice(t * P, (t + 1) * P)
                pe.wait_ge(h_lo, KD * (1 + t // 4))
                if t == 0:
                    pe.wait_ge(wv_split, KD)
                else:
                    pe.wait_ge(v_taken, 2 * t - 1)
                for k in range(KD):
                    ins = product(PS[:, 7, 0:B_H + VA_W], [a[:, k, cols] for a in act_hl],
                                  [w[:, k, VB_W:WV] for w in wv_hl], k == 0, k == KD - 1)
                ins.then_inc(v_ready, 1)
                if t >= 2:
                    pe.wait_ge(v_taken, 2 * t - 2)
                for k in range(KD):
                    ins = product(PS[:, 5 + t % 2], [a[:, k, cols] for a in act_hl],
                                  [w[:, k, 0:VB_W] for w in wv_hl], k == 0, k == KD - 1)
                ins.then_inc(v_ready, 1)

            values(0)
            pe.wait_ge(xn_ok, 2)
            for t in range(2):
                for g in range(KD + 4 * t, KD + 4 * t + 4):
                    transpose_group(g, xin[:, 4:8])
                values(t + 1)
            for t in range(3, NTOK):
                values(t)

            def project(j, first, end, bank):
                n, ch = chunks[j][:2]
                if first == 0:
                    pe.wait_ge(w_split, n + 1)
                    if j >= 4:
                        pe.wait_ge(proj_taken, j)
                for m in range(first, end):
                    k, (a, b) = m // 3, TERMS[m % 3]
                    ins = nc.tensor.matmul(PS[:, bank], w_hl[a][:, n % 2, k], act_hl[b][:, k, ch * NT:(ch + 1) * NT],
                                           start=(m == 0), stop=(m == 3 * KD - 1))
                if end == 3 * KD:
                    ins.then_inc(proj_ready, 1)

            for j in range(4):
                project(j, 0, 3 * KD, j)

            pe.wait_ge(nlf_ok, 1)
            for cc in range(CH):
                for tt in range(4):
                    t = 4 * cc + tt
                    dst = PS[0:B_H, 5 + cc, tt * P:(tt + 1) * P]
                    nc.tensor.matmul(dst, nlf[:, t], tri[:, :], start=True, stop=False)
                    ins = nc.tensor.matmul(dst, pref[:, t], ones[:, :], start=False, stop=True)
                ins.then_inc(cum_ready, 1)

            def scores(u):
                p, i, h = parts(u)
                if h == 0 and i % 4 == 0:
                    j = q_chunk[p][i // 4]
                    pe.wait_ge(rope_done if j < N_ROPE else proj_taken, j + 1)
                if u >= 2:
                    pe.wait_ge(s_taken, u - 1)
                else:
                    pe.wait_ge(proj_taken, 2 + 2 * u)
                rows = slice(h * HALF, (h + 1) * HALF)
                q = [a[rows, p % 2, i * P:(i + 1) * P] for a in q_hl]
                slot = 1 if p < 4 else p % 2
                k0, w = first_block(u) * P, width(u)
                for c0 in range(0, w, NT):
                    n = min(NT, w - c0)
                    dst = PS[:, 1 + 2 * (u % 2) + c0 // NT, 0:n]
                    keys = [a[rows, slot, k0 + c0:k0 + c0 + n] for a in k_hl]
                    for t, (a, b) in enumerate(TERMS):
                        ins = nc.tensor.matmul(dst, q[a], keys[b], start=(t == 0), stop=(t == 2))
                        if t == 0 and p >= 4 and c0 + n == w:
                            nc.tensor.matmul(dst[:, n - P:n], identb[:, :], causalb[:, :], start=False, stop=False)
                ins.then_inc(s_ready, 1)

            def free_bank(g):
                if g < 2:
                    pe.wait_ge(cum_taken, CH)
                else:
                    kind, n = group_kind[g - 2]
                    pe.wait_ge(*((grp_lo, n + 1) if kind == "p" else (grp_hi, g - 1)))

            def transpose_p(u):
                pe.wait_ge(p_ready, u + 1)
                for g, slot, blocks in p_groups[u]:
                    free_bank(g)
                    for b in blocks:
                        ins = nc.tensor.transpose(PS[:, 5 + g % 2, (b - blocks[0]) * P:(b - blocks[0] + 1) * P],
                                                  s_sb[:, u % 2, b * P:(b + 1) * P], ident[:, :])
                    ins.then_inc(grp_ready, 1)

            def times_v(u):
                p, i, h = parts(u)
                if h == 0:
                    if u == 0:
                        pe.wait_ge(v_taken, 2 * NTOK)
                    else:
                        pe.wait_ge(o_taken, u // 2)
                nb = width(u) // P
                for g, slot, blocks in p_groups[u]:
                    pe.wait_ge(grp_lo, slot + 1)
                    for b in blocks:
                        cols = slice((b - blocks[0]) * P, (b - blocks[0] + 1) * P)
                        whole, part = PS[:, 7, h * P:(h + 1) * P], PS[:, 7, h * P:h * P + HALF]
                        p_hi, p_lo = (a[:, slot % 4, cols] for a in pt_hl)
                        v_both, v_hi = (v_of(u, first_block(u) + b, lo) for lo in (False, True))
                        if nb == 1:
                            nc.tensor.matmul(whole, p_hi, v_both, start=True, stop=False)
                            ins = nc.tensor.matmul(whole, p_lo, v_both, start=False, stop=True)
                        elif b < nb - 1:
                            nc.tensor.matmul(whole, p_hi, v_both, start=(b == 0), stop=False)
                            ins = nc.tensor.matmul(part, p_lo, v_hi, start=False, stop=False)
                        else:
                            nc.tensor.matmul(part, p_lo, v_hi, start=False, stop=False)
                            ins = nc.tensor.matmul(whole, p_hi, v_both, start=False, stop=True)
                    ins.then_inc(pv_done, 1)

            scores(0)
            for u in range(NU + 2):
                if u + 1 < NU:
                    scores(u + 1)
                if u % 2 == 1 and u >= 3:
                    tile = (u - 3) // 2
                    g = o_group[tile]
                    pe.wait_ge(o_taken, tile + 1)
                    free_bank(g)
                    nc.tensor.transpose(PS[:, 5 + g % 2, 0:P], o_sb[:, tile % 2], ident[:, :]).then_inc(grp_ready, 1)
                if u < NU:
                    transpose_p(u)
                    for j, first, end in mm_at[u]:
                        project(j, first, end, 0)
                if 1 <= u <= NU:
                    times_v(u - 1)

            pe.wait_ge(proj_taken, len(chunks))
            pe.wait_ge(s_taken, NU)
            pe.wait_ge(o_taken, NU // 2)
            pe.wait_ge(grp_hi, len(group_kind))
            pe.wait_ge(grp_lo, np_groups)
            with pe.Fori(0, KD // 2) as it:
                for mm in range(2):
                    for r in range(3):
                        n = N_ATT + 3 * mm + r
                        pe.wait_ge(w_split, it * 6 + (n + 1))
                        if r < 2:
                            for ch in range(CH):
                                j = 2 * r + ch
                                if j < 3:
                                    pe.wait_ge(g_done, it * 8 + (4 * mm + j + 1))
                                else:
                                    pe.wait_ge(br_taken, it * 8 + (4 * mm + 4))
                                for k in range(KD):
                                    ins = product(PS[:, j], [w[:, n % 2, k] for w in w_hl],
                                                  [a[:, k, ch * NT:(ch + 1) * NT] for a in act_hl], k == 0, k == KD - 1)
                                ins.then_inc(g_ready, 1)
                        else:
                            pe.wait_ge(ob_split, 8)
                            for j in range(4):
                                ch = j % 2
                                if j < 3:
                                    pe.wait_ge(br_taken, it * 8 + (4 * mm + j + 1))
                                else:
                                    pe.wait_ge(g_done, it * 8 + (4 * mm + 8))
                                for kk in range(4):
                                    k = 4 * (j // 2) + kk
                                    ins = product(PS[:, BR_BANK[j]], [w[:, n % 2, k] for w in w_hl],
                                                  [a[:, k, ch * NT:(ch + 1) * NT] for a in ob_hl], kk == 0, kk == 3)
                                ins.then_inc(br_ready, 1)
                        for q in ((0,), (1,), (2, 3))[r]:
                            a = 4 * mm + q
                            pe.wait_ge(ada2_in[a % 2], it * 64 + 16 * (a // 2 + 1))
                            for k in range(KD):
                                ins = nc.tensor.matmul(PS[:, 7, bass.ds(it * 8 + a, 1)], adaraw[:, a % 2, k],
                                                       pcols[:, k:k + 1], start=(k == 0), stop=(k == KD - 1))
                            ins.then_inc(ada_used, 1)

            def out_proj(t, k):
                b = y_bank(t)
                for hb in range(2):
                    ins = product(PS[:, b + hb], [a[:, k, t * P:(t + 1) * P] for a in act_hl],
                                  [w[:, k, hb * NT:(hb + 1) * NT] for w in ob_hl], k == 0, k == KD - 1)
                if k == KD - 1:
                    ins.then_inc(y_ready, 1)

            pe.wait_ge(g_done, 4 + 4 * KD)
            pe.wait_ge(br_taken, 4 + 4 * KD)
            for k in range(KD):
                pe.wait_ge(wo_split, k + 1)
                pe.wait_ge(m_split, k + 1)
                for t in range(3):
                    out_proj(t, k)
                if k >= 4:
                    r = k - 4
                    pe.wait_ge(diag_ok, r + 1)
                    if r >= 2:
                        pe.wait_ge(grow_ok, r - 1)
                    nc.tensor.matmul(PS[:, 6 + r % 2], ones[:, :], diag[:, :, :].rearrange("p a n -> p (a n)"),
                                     start=True, stop=True).then_inc(grow_ready, 1)
            pe.wait_ge(m_split, 2 * KD)
            for t in range(3, NTOK):
                if t == 3:
                    pe.wait_ge(grow_ok, 4)
                else:
                    pe.wait_ge(y_taken, {4: 1, 5: 3, 6: 4, 7: 5}[t])
                if t == 5:
                    pe.wait_ge(xn_ok, 2 + 4)
                    pe.wait_ge(y_taken, 2)
                for k in range(KD):
                    out_proj(t, k)
                    if t == 5:
                        transpose_group(2 * KD + k, xn)
            pe.wait_ge(xn_ok, 2 + NTOK)
            for k in range(KD):
                transpose_group(3 * KD + k, xn)

            pe.wait_ge(h_lo, 4 * KD)
            pe.wait_ge(y_taken, NTOK)
            with pe.Fori(0, FT // 2) as it:
                for ff in range(2):
                    for j in range(2):
                        n = N_FF + 2 * ff + j
                        pe.wait_ge(w_split, it * 4 + (n + 1))
                        for ch in range(CH):
                            if j == 0 and ch == 0:
                                pe.wait_ge(ff_ok, it * 4 + (2 * ff + 2))
                            for k in range(KD):
                                ins = product(PS[:, 4 * ff + 2 * j + ch], [w[:, n % 2, k] for w in w_hl],
                                              [a[:, k, ch * NT:(ch + 1) * NT] for a in act_hl], k == 0, k == KD - 1)
                            ins.then_inc(ff_ready, 1)

            def down(t, j, first, last):
                return product(PS[:, t], [a[:, j, t * P:(t + 1) * P] for a in ah_hl], [w[:, j] for w in w2_hl], first, last)

            pe.wait_ge(ff_ok, 4 + 2 * FT)
            for half in range(2):
                def operands(it, j):
                    pe.wait_ge(ah_split, it * 2 + (FT * half + j + 1))
                    pe.wait_ge(w2_split, it * 2 + (FT * half + j + 3))

                for j in range(2):
                    operands(0, j)
                    for t in range(NTOK):
                        if half == 1 and j == 0:
                            pe.wait_ge(z_taken, t + 1)
                        ins = down(t, j, j == 0, False)
                        if half == 1 and j == 0 and t == 0:
                            ins.then_inc(ah_used, 1)
                    ins.then_inc(ah_used, 1)
                with pe.Fori(1, FT // 2 - 1) as it:
                    for j in range(2):
                        operands(it, j)
                        for t in range(NTOK):
                            ins = down(t, j, False, False)
                        ins.then_inc(ah_used, 1)
                if half == 0:
                    for j in range(2):
                        operands(FT // 2 - 1, j)
                        for t in range(NTOK):
                            ins = down(t, j, False, j == 1)
                            if j == 1:
                                ins.then_inc(z_ready, 1)
                        if j == 0:
                            ins.then_inc(ah_used, 1)
                else:
                    for j in range(2):
                        operands(FT // 2 - 1, j)
                    for t in range(NTOK):
                        for j in range(2):
                            ins = down(t, j, False, j == 1)
                        ins.then_inc(z_ready, 1)


_INS = ["x", "c", "positions", "w_ada", "b_ada", "g_pre_mix", "g_post_mix", "w_in", "b_f", "sinks", "w_branch_a",
        "w_branch_b", "w_out", "g_pre_ffn", "g_post_ffn", "w_ffn_in", "w_ffn_out"]
_OUT = ((1, 1024, 1024), "float32")


def _inverse_frequencies():
    import numpy as np
    half = np.arange(0, 64, 2, dtype=np.float32) / np.float32(64)
    return np.tile(np.float32(1.0) / (np.float32(10000.0) ** half), 4).reshape(128, 1).astype(np.float32)


def kernel(**inputs):
    import numpy as np
    import concourse.bacc as bacc
    from concourse import mybir as mb
    from concourse.bass_utils import run_bass_kernel_spmd as run

    nc = bacc.Bacc("TRN2", target_bir_lowering=False, num_devices=1, dynamic_dma_scratch_size=1024)
    arrays, args = {}, []

    def give(name, a):
        arrays[f"in_{name}_dram"] = a
        args.append(nc.dram_tensor(f"in_{name}_dram", a.shape, mb.dt.from_np(a.dtype), kind="ExternalInput").ap())

    for name in _INS:
        give(name, np.ascontiguousarray(inputs[name]))
    give("inv_freq", _inverse_frequencies())
    args.append(nc.dram_tensor("out_0_dram", _OUT[0], mb.dt.from_np(np.dtype(_OUT[1])), kind="ExternalOutput").ap())
    hybrid_layer(nc, *args)
    return run(nc, [arrays], core_ids=[0]).results[0]["out_0_dram"]
```

```python
from contextlib import ExitStack
import math

import concourse.bass as bass
from concourse import mybir

F32 = mybir.dt.float32
F32R = mybir.dt.float32r
BF16 = mybir.dt.bfloat16
I32 = mybir.dt.int32
ALU = mybir.AluOpType
ACT = mybir.ActivationFunctionType

P = 128
HALF = 64
NT = 512
EPS = 1e-6
BIG = 3.0e38
MASKED = -1.0e30
ROUND = 1.5 * 2.0 ** 23
TURN = (6.28125, 0.0019350051879882812, 3.019813448190689e-07, 1.0253376273028358e-11)
PI_BELOW = 3.1415925
BR_BANK = (4, 5, 6, 3)
TERMS = ((0, 0), (0, 1), (1, 0))


def hybrid_layer(nc, x, c, positions, w_ada, b_ada, g_pre_mix, g_post_mix, w_in, b_f, sinks,
                 w_branch_a, w_branch_b, w_out, g_pre_ffn, g_post_ffn, w_ffn_in, w_ffn_out,
                 inv_freq, out):
    S, D = x.shape[1], x.shape[2]
    NTOK = S // P
    KD = D // P
    CH = S // NT
    FT = w_ffn_out.shape[1] // P
    DFF = FT * P
    HD = HALF
    A_Q, A_KV, B_H = sinks.shape[1], 2, b_f.shape[1]
    C_QA = 0
    C_KA = C_QA + A_Q * HD
    C_VA = C_KA + A_KV * HD
    C_QB = C_VA + A_KV * HD
    C_KB = C_QB + B_H * HD
    C_VB = C_KB + B_H * HD
    C_F = C_VB + B_H * HD
    C_G = C_F + B_H
    VB_W, VA_W = B_H * HD, A_KV * HD
    WV = VB_W + B_H + VA_W
    SM = 1.0 / math.sqrt(HD)
    assert (S, D, HD, VB_W, A_Q, B_H) == (1024, 1024, 64, 512, 8, 8)

    oT_dram = nc.dram_tensor("oT_dram", (8, P, S), F32, kind="Internal").ap()
    x1_dram = nc.dram_tensor("x1_dram", (NTOK, P, D), F32, kind="Internal").ap()
    ncum_dram = nc.dram_tensor("ncum_dram", (B_H, S), F32, kind="Internal").ap()

    base = (nc.sbuf_base + 63) // 64 * 64
    KB = 1024

    def at(name, off, shape, dt=F32):
        return nc.alloc_sbuf_tensor_at(name, shape, dt, offset=base + off)

    cursor = [0]

    def small(name, shape, dt=F32):
        size = 2 if dt == BF16 else 4
        for n in shape[1:]:
            size *= n
        o = cursor[0]
        cursor[0] += (size + 31) // 32 * 32
        return at(name, o, shape, dt)

    ident = small("ident", [P, P])
    tri = small("tri", [P, P])
    ones = small("ones", [P, P])
    band = small("band", [P, 2 * P])
    identb = small("identb", [P, P], BF16)
    causalb = small("causalb", [P, P], BF16)
    pcols = small("pcols", [P, 88])
    adac = small("adac", [P, 48])
    a_mix = small("a_mix", [P, KD])
    a_ffn = small("a_ffn", [P, KD])
    gm_col = small("gm_col", [P, 2 * KD])
    invf = small("invf", [P, 1])
    sgn = small("sgn", [P, 1])
    bfb = small("bfb", [P, B_H])
    sinkb = small("sinkb", [P, A_Q])
    nsink = small("nsink", [P, A_Q])
    nmax = small("nmax", [P, 8])
    den = small("den", [P, 8])
    rden = small("rden", [P, 2, 2])
    ot = small("ot", [P, 2, 2, HALF])
    ssq = small("ssq", [P, 32])
    z = small("z", [P, NTOK, B_H])
    credit = small("credit", [P, 8])
    scratch = small("scratch", [P, 1])
    ssq_b = small("ssq_b", [P, NTOK])
    var = small("var", [P, 32])
    rms = small("rms", [P, 32])
    rstd = small("rstd", [P, 32])
    P_END = (cursor[0] + 63) // 64 * 64
    H0 = P_END
    W0 = H0 + 64 * KB
    R0 = W0 + 24 * KB
    R_SIZE = nc.sbuf_usable_end - base - R0
    assert R_SIZE >= int(128.5 * KB), R_SIZE

    act_hl = [at(f"act_{s}", H0 + i * 32 * KB, [P, KD, S], F32R) for i, s in enumerate(("hi", "lo"))]
    wraw = at("wraw", W0, [P, 2, KD, P])
    w_hl = [at(f"w_{s}", W0 + (1 + i) * 8 * KB, [P, 2, KD, P], F32R) for i, s in enumerate(("hi", "lo"))]
    CS = 72 * KB + 8 * KD * WV
    wada = at("wada", R0, [P, 2, KD, NT])
    ada_acc = at("ada_acc", R0 + CS + 8 * KB, [P, 2, NT])
    posi = at("posi", R0 + CS + 4 * KB, [P, S], I32)
    ang = at("ang", R0 + 24 * KB, [P, S])
    turns = at("turns", R0 + 28 * KB, [P, S])
    wv_hl = [at(f"wv_{s}", R0 + 72 * KB + i * 4 * KD * WV, [P, KD, WV], F32R) for i, s in enumerate(("hi", "lo"))]
    wvraw = at("wvraw", W0, [P, KD, WV])
    xin = at("xin", R0 + 40 * KB, [P, NTOK, D])
    cs = at("cs", R0 + CS, [P, 2, 2, S])
    htmp = at("htmp", R0 + CS + 8 * KB, [P, 2, NT])
    junk = at("junk", R0 + CS + 12 * KB, [P, D])
    prow = at("prow", H0, [88, P])
    vb_hl = at("vb_hl", R0, [P, NTOK, B_H, 2, HD], F32R)
    va_hl = at("va_hl", R0 + 32 * KB, [P, NTOK, A_KV, 2, HD], F32R)
    q_hl = [at(f"q_{s}", R0 + (40 + 8 * i) * KB, [P, 2, S], F32R) for i, s in enumerate(("hi", "lo"))]
    k_hl = [at(f"k_{s}", R0 + (56 + 8 * i) * KB, [P, 2, S], F32R) for i, s in enumerate(("hi", "lo"))]
    s_sb = at("s_sb", R0 + 72 * KB, [P, 2, S])
    s_sb2 = at("s_sb2", R0 + 96 * KB, [P, S])
    pt_hl = [at(f"pt_{s}", R0 + (80 + 8 * i) * KB, [P, 4, NT], F32R) for i, s in enumerate(("hi", "lo"))]
    rope_a = at("rope_a", R0 + CS + 8 * KB, [P, NT])
    rope_b = at("rope_b", R0 + CS + 10 * KB, [P, NT])
    ostage = at("ostage", R0 + 100 * KB, [P, 4, P])
    o_sb = at("o_sb", R0 + 102 * KB, [P, 2, P])
    fg = [at(f"fg{i}", R0 + 103 * KB + 256 * i, [P, NTOK, B_H]) for i in range(7)]
    absz, ez, onep, lnp, corr, nlf, pref = fg
    ncum = at("ncum", R0 + 106 * KB, [B_H, S])
    ob_hl = [at(f"ob_{s}", R0 + 32 * i * KB, [P, KD, S], F32R) for i, s in enumerate(("hi", "lo"))]
    merged = at("merged", R0 + 64 * KB, [P, KD, S])
    sg = at("sg", R0 + 96 * KB, [P, 4, NT])
    adaraw = at("adaraw", R0 + CS - 8 * KB, [P, 2, KD, P])
    ada_acc2 = at("ada_acc2", R0 + CS, [P, 2, P])
    grow = at("grow", R0 + CS, [P, 2, D])
    woraw = at("woraw", R0 + CS + 8 * KB, [P, 2, D])
    xr = at("xr", R0 + 64 * KB, [P, 2, D])
    x1 = at("x1", R0 + 72 * KB, [P, 2, D])
    xn = at("xn", R0 + 80 * KB, [P, 4, D])
    htmp2 = at("htmp2", R0 + 96 * KB, [P, 2, NT])
    junk2 = at("junk2", R0 + 100 * KB, [P, D])
    junk_x = at("junk_x", R0 + CS + 8 * KB, [P, D])
    diag = at("diag", R0 + 96 * KB, [P, 4, P])
    act_ff = at("act_ff", R0, [P, FT, S])
    sl = at("sl", R0 + CS - 8 * KB, [P, 4, NT])
    w2raw = at("w2raw", R0 + 88 * KB, [P, 2, NT])
    w2_hl = [at(f"w2_{s}", R0 + (92 + 4 * i) * KB, [P, 2, NT], F32R) for i, s in enumerate(("hi", "lo"))]
    ah_hl = [at(f"ah_{s}", H0 + 8 * i * KB, [P, 2, S], F32R) for i, s in enumerate(("hi", "lo"))]
    y0 = at("y0", H0 + 16 * KB, [P, NTOK, NT])
    x1r = at("x1r", H0 + 32 * KB, [P, 4, D])
    fin = at("fin", H0 + 48 * KB, [P, 2, D])
    junk3 = at("junk3", H0 + 56 * KB, [P, D])

    PAIRS = 8
    NU = PAIRS * NTOK * 2

    def parts(u):
        return u // 16, (u % 16) // 2, u % 2

    def width(u):
        p, i, _ = parts(u)
        return P * (min(i + 1, 2) if p < 4 else i + 1)

    def first_block(u):
        p, i, _ = parts(u)
        return max(i - 1, 0) if p < 4 else 0

    def scores_slot(u):
        return s_sb[:, u % 3] if u % 3 < 2 else s_sb2[:, :]

    def v_of(u, blk, lo):
        p, _, h = parts(u)
        v = va_hl[:, blk, h] if p < 4 else vb_hl[:, blk, 2 * (p - 4) + h]
        return v[:, 0] if lo else v.rearrange("p a d -> p (a d)")

    p_groups = {}
    o_group = {}
    group_kind = []
    np_groups = 0
    for u in range(NU + 3):
        if u < NU:
            nb = width(u) // P
            p_groups[u] = []
            for b0 in range(0, nb, 4):
                p_groups[u].append((len(group_kind), np_groups, range(b0, min(b0 + 4, nb))))
                group_kind.append(("p", np_groups))
                np_groups += 1
        if u % 2 == 0 and u >= 4:
            o_group[(u - 4) // 2] = len(group_kind)
            group_kind.append(("o", (u - 4) // 2))

    chunks = [(0, 0, k_hl, 1, "rope"), (0, 1, k_hl, 1, "rope"), (1, 0, q_hl, 0, "rope"), (1, 1, q_hl, 0, "rope")]
    CUM_STEP = 2
    mm_at = {u: [] for u in range(NU)}
    evac_at = {u: [] for u in range(NU)}
    chunk_bank = [0, 1, 2, 3]
    q_chunk = {0: (2, 3)}
    for p in range(PAIRS - 1):
        if p < 3:
            q_chunk[p + 1] = (len(chunks), len(chunks) + 1)
            for ch in range(CH):
                first, steps = 6 * ch, 6 + 4 * ch
                for s in range(steps):
                    mm_at[16 * p + first + s].append((len(chunks), 3 * KD * s // steps, 3 * KD * (s + 1) // steps))
                for part in range(4):
                    evac_at[16 * p + first + steps + part].append((len(chunks), part))
                chunk_bank.append(2 * ((len(chunks) + 1) % 2))
                chunks.append((p + 2, ch, q_hl, (p + 1) % 2, "rope"))
        else:
            q_chunk[p + 1] = (len(chunks) + 2, len(chunks) + 3)
            for j in range(4):
                steps = 4 if p == 3 or j == 0 else 3
                per = 3 * KD // steps
                for s in range(steps):
                    mm_at[16 * p + 4 * j + s].append((len(chunks), per * s, per * s + per))
                evac_at[16 * p + 4 * j + steps].append((len(chunks), 0))
                chunk_bank.append(2 if j % 2 == 0 and (p == 3 or j == 0) else 0)
                chunks.append((5 + 2 * (p - 3) + j // 2, j % 2, (k_hl, q_hl)[j // 2], (p + 1) % 2, "plain"))
    N_ROPE = 10
    N_ATT = 13
    N_BR = 3 * KD
    N_FF = N_ATT + N_BR
    N_ADA = 4 * KD

    def h_bank(g):
        return g % 4 if g < 2 * KD else 2 + g % 2

    def y_bank(t):
        return (0, 2, 4, 6, 0, 4, 6, 0)[t]

    MIX_ORDER = [("residual", 0), ("residual", 1), ("norm", 0), ("residual", 2), ("norm", 1), ("norm", 2),
                 ("residual", 3), ("norm", 3), ("half", 0)]
    for t in range(4, NTOK):
        MIX_ORDER += [("residual", t), ("norm", t)]
    MIX_ORDER.append(("half", 1))

    with ExitStack() as ctx:
        PS = ctx.enter_context(nc.psum_tensor("PS", [P, 8, NT], F32))

        def sem(name):
            return ctx.enter_context(nc.semaphore(name))

        par_in, bc_in = sem("par_in"), sem("bc_in")
        x_in = [sem("x_in0"), sem("x_in1")]
        ada_in = [sem("ada_in0"), sem("ada_in1")]
        ada2_in = [sem("ada2_in0"), sem("ada2_in1")]
        wv_in = [sem(f"wv_in{k}") for k in range(KD)]
        w_in_s = [sem("w_in_s0"), sem("w_in_s1")]
        cum_in = [sem("cum_in0"), sem("cum_in1")]
        const_ok = sem("const_ok")
        prow_ready, pcols_ok = sem("prow_ready"), sem("pcols_ok")
        ada_used, ada_taken, acc_ready = sem("ada_used"), sem("ada_taken"), sem("acc_ready")
        ada_prod = sem("ada_prod")
        xt_ready, h_hi, h_tmp, h_lo = sem("xt_ready"), sem("h_hi"), sem("h_tmp"), sem("h_lo")
        ssq_ok, var_ok, rms_ok, rstd_ok, xn_ok = (sem("ssq_ok"), sem("var_ok"), sem("rms_ok"), sem("rstd_ok"),
                                                  sem("xn_ok"))
        reduced, tables = sem("reduced"), sem("tables")
        wv_hi_ok, wv_split = sem("wv_hi_ok"), sem("wv_split")
        v_ready, v_hi_ok, v_taken = sem("v_ready"), sem("v_hi_ok"), sem("v_taken")
        absz_ok, ez_ok, onep_ok, lnp_ok, nlf_ok = sem("absz_ok"), sem("ez_ok"), sem("onep_ok"), sem("lnp_ok"), sem("nlf_ok")
        cum_ready, cum_taken, cum_out = sem("cum_ready"), sem("cum_taken"), sem("cum_out")
        w_hi_ok, w_split = sem("w_hi_ok"), sem("w_split")
        proj_ready, proj_hi, proj_taken = sem("proj_ready"), sem("proj_hi"), sem("proj_taken")
        rope_sum, rope_hi, rope_done = sem("rope_sum"), sem("rope_hi"), sem("rope_done")
        s_ready, s_taken, p_ready = sem("s_ready"), sem("s_taken"), sem("p_ready")
        grp_ready, grp_hi, grp_lo = sem("grp_ready"), sem("grp_hi"), sem("grp_lo")
        pv_done, o_taken, rden_ok, o_ok = sem("pv_done"), sem("o_taken"), sem("rden_ok"), sem("o_ok")
        o_out = [sem(f"o_out{i}") for i in range(4)]
        dve_step, pool_step, act_step = sem("dve_step"), sem("pool_step"), sem("act_step")
        ob_in, ob_hi_ok, ob_split = sem("ob_in"), sem("ob_hi_ok"), sem("ob_split")
        g_ready, g_done = sem("g_ready"), sem("g_done")
        br_ready, br_taken, merged_ok = sem("br_ready"), sem("br_taken"), sem("merged_ok")
        wo_in = [sem("wo_in0"), sem("wo_in1")]
        wo_hi_ok, wo_split, m_hi_ok, m_split = sem("wo_hi_ok"), sem("wo_split"), sem("m_hi_ok"), sem("m_split")
        gcol_ok, diag_ok, grow_ready, grow_ok = sem("gcol_ok"), sem("diag_ok"), sem("grow_ready"), sem("grow_ok")
        xr_in = [sem("xr_in0"), sem("xr_in1")]
        x1_out = [sem("x1_out0"), sem("x1_out1")]
        y_ready, y_sq, y_var, y_rms = sem("y_ready"), sem("y_sq"), sem("y_var"), sem("y_rms")
        y_taken, x1_ok, x1_sq, x1_var, x1_rms = (sem("y_taken"), sem("x1_ok"), sem("x1_sq"), sem("x1_var"),
                                                          sem("x1_rms"))
        ff_ready, silu_ok, ff_ok = sem("ff_ready"), sem("silu_ok"), sem("ff_ok")
        w2_in = [sem("w2_in0"), sem("w2_in1")]
        w2_hi_ok, w2_split = sem("w2_hi_ok"), sem("w2_split")
        ah_hi_ok, ah_split, ah_used = sem("ah_hi_ok"), sem("ah_split"), sem("ah_used")
        z_ready, z_taken, z_sq, z_var, z_rms, fin_ok = (sem("z_ready"), sem("z_taken"), sem("z_sq"), sem("z_var"),
                                                        sem("z_rms"), sem("fin_ok"))
        x1r_in = [sem(f"x1r_in{i}") for i in range(4)]
        done = [sem("done0"), sem("done1")]

        block = ctx.enter_context(nc.Block())

        w_in_v = w_in[0].rearrange("(k p) n -> p k n", p=P)
        w_ada_v = w_ada[0].rearrange("(k p) n -> p k n", p=P)
        w_out_v = w_out[0].rearrange("(k p) n -> k p n", p=P)
        w_a_v = w_branch_a[0].rearrange("(f g d) n -> f d g n", f=2, d=HD)
        w_b_v = w_branch_b[0].rearrange("(k p) n -> p k n", p=P)
        w_fi_v = w_ffn_in[0].rearrange("(k p) n -> p k n", p=P)
        w_fo_v = w_ffn_out[0].rearrange("(k p) n -> p k n", p=P)
        x_v = x[0].rearrange("(t p) d -> t p d", p=P)
        out_v = out[0].rearrange("(t p) d -> t p d", p=P)

        UNIT = 48

        @block.sync
        def _(sp):
            at_row = 0
            for src in (c, b_ada, g_pre_mix, g_post_mix, g_pre_ffn, g_post_ffn):
                n = src.shape[1] // P
                sp.dma_start(prow[at_row:at_row + n, :], src[0].rearrange("(r p) -> r p", p=P)).then_inc(par_in, 16)
                at_row += n
            sp.dma_start(bfb[:, :], b_f[0].partition_broadcast(P)).then_inc(bc_in, 16)
            sp.dma_start(sinkb[:, :], sinks[0].partition_broadcast(P)).then_inc(bc_in, 16)
            sp.dma_start(posi[:, :], positions[0].partition_broadcast(P)).then_inc(bc_in, 16)
            sp.dma_start(invf[:, :], inv_freq).then_inc(bc_in, 16)
            for j in range(4):
                if j >= 2:
                    sp.wait_ge(acc_ready, j - 1)
                sp.dma_start(wada[:, j % 2], w_ada_v[:, :, j * NT:(j + 1) * NT]).then_inc(ada_in[j % 2], 16)
                if j == 0:
                    for t in range(4):
                        sp.dma_start(xin[:, t, :], x_v[t]).then_inc(x_in[0], 16)
            for k in range(KD):
                sp.dma_start(wvraw[:, k, 0:VB_W + B_H], w_in_v[:, k, C_VB:C_VB + VB_W + B_H]).then_inc(wv_in[k], 16)
                sp.dma_start(wvraw[:, k, VB_W + B_H:WV], w_in_v[:, k, C_VA:C_VA + VA_W]).then_inc(wv_in[k], 16)
            for t in range(4, 8):
                sp.dma_start(xin[:, t, :], x_v[t]).then_inc(x_in[1], 16)

            sp.wait_ge(wv_split, KD)
            for n in range(N_ATT):
                if n >= 2:
                    sp.wait_ge(w_split, n - 1)
                if n == 0:
                    sp.dma_start(wraw[:, 0], w_in_v[:, :, C_KA:C_KA + P]).then_inc(w_in_s[0], UNIT)
                elif n < 5:
                    for f, col in enumerate((C_QA + (n - 1) * HD, C_QA + (n + 3) * HD)):
                        sp.dma_start(wraw[:, n % 2, :, f * HD:(f + 1) * HD],
                                     w_in_v[:, :, col:col + HD]).then_inc(w_in_s[n % 2], 16 + 16 * f)
                else:
                    col = (C_KB, C_QB)[(n - 5) % 2] + (n - 5) // 2 * P
                    sp.dma_start(wraw[:, n % 2], w_in_v[:, :, col:col + P]).then_inc(w_in_s[n % 2], UNIT)
                if n > 5 and n % 2 == 0:
                    p = 4 + (n - 5) // 2
                    slot = 1 - p % 2
                    if p == 4:
                        sp.wait_ge(cum_taken, CH)
                        sp.dma_start(ncum_dram, ncum[:, :]).then_inc(cum_out, 16)
                        sp.wait_ge(cum_out, 16)
                        sp.wait_ge(rope_done, N_ROPE)
                    elif p == 5:
                        sp.wait_ge(proj_taken, N_ROPE)
                    else:
                        sp.wait_ge(s_taken, 16 * (p - 1))
                    sp.dma_start(cs[:, slot], ncum_dram[2 * (p - 4):2 * (p - 4) + 2, :].partition_broadcast(P))\
                        .then_inc(cum_in[slot], 16)

            with sp.Fori(1, KD // 2 + 1) as it:
                for mm in range(2):
                    col = it * (2 * P) + (mm - 2) * P
                    for j in range(3):
                        n = N_ATT + 3 * mm + j
                        src = w_in_v[:, :, bass.ds(col + (C_G + j * D), P)] if j < 2 else None
                        sp.wait_ge(w_split, it * 6 + (n - 1 - 6))
                        if j < 2:
                            sp.dma_start(wraw[:, n % 2], src)\
                                .then_inc(w_in_s[n % 2], UNIT)
                        else:
                            for f in range(2):
                                sp.dma_start(wraw[f * HD:(f + 1) * HD, n % 2, 0:4, :], w_a_v[f, :, :, bass.ds(col, P)])\
                                    .then_inc(w_in_s[n % 2], 16)
                            sp.dma_start(wraw[:, n % 2, 4:8, :], w_b_v[:, :, bass.ds(col, P)]).then_inc(w_in_s[n % 2], 16)
                        for q in ((0,), (1,), (2, 3))[j]:
                            a = 4 * mm + q
                            sp.wait_ge(acc_ready, it * 8 + (a + 3 - 8))
                            sp.dma_start(adaraw[:, a % 2], w_ada_v[:, :, bass.ds(it * (8 * P) + (16 * P + (a - 8) * P), P)])\
                                .then_inc(ada2_in[a % 2], 16)

            for k in range(KD):
                if k >= 2:
                    sp.wait_ge(wo_split, k - 1)
                sp.dma_start(woraw[:, k % 2], w_out_v[k]).then_inc(wo_in[k % 2], 16)
            for n in (N_FF, N_FF + 1):
                sp.wait_ge(w_split, n - 1)
                col = (n - N_FF) * DFF
                sp.dma_start(wraw[:, n % 2], w_fi_v[:, :, col:col + P]).then_inc(w_in_s[n % 2], UNIT)
            sp.wait_ge(m_split, 2 * KD)
            for t in range(2):
                sp.dma_start(xr[:, t], x_v[t]).then_inc(xr_in[t], 16)
            for t in range(NTOK):
                sp.wait_ge(x1_ok, t + 1)
                sp.dma_start(x1_dram[t], x1[:, t % 2]).then_inc(x1_out[t % 2], 16)
                if t + 2 < NTOK:
                    sp.dma_start(xr[:, t % 2], x_v[t + 2]).then_inc(xr_in[t % 2], 16)

            with sp.Fori(0, FT - 1) as it:
                for j in range(2):
                    n = N_FF + 2 + j
                    sp.wait_ge(w_split, it * 2 + (n - 1))
                    sp.dma_start(wraw[:, n % 2], w_fi_v[:, :, bass.ds(it * P + (P + j * DFF), P)])\
                        .then_inc(w_in_s[n % 2], UNIT)
            sp.wait_ge(xn_ok, 2 + NTOK)
            for half in range(2):
                with sp.Fori(0, FT // 2) as it:
                    for j in range(2):
                        sp.wait_ge(w2_split, it * 2 + (FT * half + j + 1))
                        sp.dma_start(w2raw[:, j], w_fo_v[:, bass.ds(it * 2 + j, 1), half * NT:(half + 1) * NT]
                                     .rearrange("p a n -> p (a n)")).then_inc(w2_in[j], 16)
                if half == 0:
                    sp.wait_ge(ff_ready, 4 * FT)
                    for i in range(2):
                        sp.wait_ge(x1_out[i], 16 * (NTOK // 2))
                    for t in range(4):
                        sp.dma_start(x1r[:, t], x1_dram[t]).then_inc(x1r_in[t], 16)
            for t in range(NTOK):
                sp.wait_ge(fin_ok, t + 1)
                sp.dma_start(out_v[t], fin[:, t % 2]).then_inc(done[t % 2], 16)
                if t + 4 < NTOK:
                    sp.dma_start(x1r[:, t % 4], x1_dram[t + 4]).then_inc(x1r_in[t % 4], 16)
            for i in range(2):
                sp.wait_ge(done[i], 16 * (NTOK // 2))

        @block.gpsimd
        def _(pool):
            step = [0]

            def link(ins):
                step[0] += 1
                ins.then_inc(pool_step, 1)
                pool.wait_ge(pool_step, step[0])

            link(pool.memset(ident[:, :], 0.0))
            link(pool.memset(ones[:, :], 1.0))
            link(pool.memset(band[:, :], 0.0))
            link(pool.affine_select(out=ident[:, :], in_=ident[:, :], compare_op=ALU.not_equal, fill=1.0,
                                    base=0, pattern=[[-1, P]], channel_multiplier=1))
            link(pool.affine_select(out=tri[:, :], in_=ones[:, :], compare_op=ALU.is_ge, fill=0.0,
                                    base=0, pattern=[[1, P]], channel_multiplier=-1))
            link(pool.affine_select(out=band[:, 0:P], in_=band[:, 0:P], compare_op=ALU.is_gt, fill=MASKED,
                                    base=0, pattern=[[1, P]], channel_multiplier=-1))
            link(pool.affine_select(out=band[:, P:2 * P], in_=band[:, P:2 * P], compare_op=ALU.is_ge, fill=MASKED,
                                    base=0, pattern=[[-1, P]], channel_multiplier=1))
            link(pool.tensor_copy(identb[:, :], ident[:, :]))
            link(pool.tensor_copy(causalb[:, :], band[:, P:2 * P]))
            for q in range(4):
                link(pool.memset(sgn[32 * q:32 * q + 32, :], 1.0 - 2.0 * (q % 2)))
            pool.memset(scratch[:, :], 0.0).then_inc(const_ok, 1)

            for k in range(KD):
                pool.wait_ge(wv_hi_ok, k + 1)
                pool.tensor_tensor(wv_hl[1][:, k], wvraw[:, k], wv_hl[0][:, k].bitcast(F32), ALU.subtract)\
                    .then_inc(wv_split, 1)

            def take_wait():
                pool.tensor_tensor(scratch[:, :], ones[:, 0:1], ones[:, 0:1], ALU.mult)

            def split_unit(slot, loads, n, att=False):
                pool.wait_ge(w_in_s[slot], loads)
                if not att:
                    take_wait()
                pool.tensor_copy(w_hl[0][:, slot], wraw[:, slot]).then_inc(w_hi_ok, 1)
                pool.wait_ge(w_hi_ok, n + 1)
                pool.tensor_tensor(w_hl[1][:, slot], wraw[:, slot], w_hl[0][:, slot].bitcast(F32), ALU.subtract)\
                    .then_inc(w_split, 1)

            def split_att(n):
                if n >= 2:
                    pool.wait_ge(proj_ready, 2 * (n - 1))
                split_unit(n % 2, UNIT * (n // 2 + 1), n, att=True)

            def rope_chunk(j):
                n, ch, dst, slot, _ = chunks[j]
                cols = slice(ch * NT, (ch + 1) * NT)
                pool.wait_ge(proj_taken, j + 1)
                pool.tensor_tensor(rope_a[:, :], rope_a[:, :], rope_b[:, :], ALU.add).then_inc(rope_sum, 1)
                pool.wait_ge(rope_sum, j + 1)
                if j >= 4:
                    pool.wait_ge(s_ready, 16 * (n - 2))
                pool.tensor_copy(dst[0][:, slot, cols], rope_a[:, :]).then_inc(rope_hi, 1)
                pool.wait_ge(rope_hi, j + 1)
                pool.tensor_tensor(dst[1][:, slot, cols], rope_a[:, :], dst[0][:, slot, cols].bitcast(F32),
                                   ALU.subtract).then_inc(rope_done, 1)

            split_att(0)
            split_att(1)
            for j in range(N_ROPE):
                rope_chunk(j)
                if j % 2 == 1:
                    split_att(chunks[j][0] + 2)
            for n in range(7, N_ATT):
                split_att(n)
            pool.wait_ge(proj_ready, len(chunks))
            with pool.Fori(0, KD // 2) as it:
                for mm in range(2):
                    for r in range(3):
                        n = N_ATT + 3 * mm + r
                        if r == 0:
                            pool.wait_ge(g_ready, it * 8 + (4 * mm + 4))
                        elif r == 1:
                            pool.wait_ge(br_ready, it * 8 + (4 * mm + 4))
                        else:
                            pool.wait_ge(g_ready, it * 8 + (4 * mm + 6))
                        split_unit(n % 2, it * (3 * UNIT) + UNIT * (n // 2 + 1), it * 6 + n)
            for n, last_use in ((N_FF, g_ready), (N_FF + 1, br_ready)):
                pool.wait_ge(last_use, 4 + 4 * KD)
                split_unit(n % 2, UNIT * (n // 2 + 1), n)
            for g in range(2 * KD, 4 * KD):
                k, half = g % KD, g // KD % 2
                cols = slice(half * NT, (half + 1) * NT)
                pool.wait_ge(h_tmp, g + 1)
                pool.tensor_tensor(act_hl[1][:, k, cols], htmp2[:, g % 2], act_hl[0][:, k, cols].bitcast(F32), ALU.subtract)\
                    .then_inc(h_lo, 1)
            for j in range(2):
                pool.wait_ge(ff_ready, 3 + j)
                n = N_FF + 2 + j
                split_unit(n % 2, UNIT * (n // 2 + 1), n)
            with pool.Fori(1, FT - 1) as it:
                for j in range(2):
                    n = N_FF + 2 + j
                    pool.wait_ge(ff_ready, it * 4 + (2 * j + 2))
                    split_unit(n % 2, it * UNIT + UNIT * (n // 2 + 1), it * 2 + n)
            for half in range(2):
                with pool.Fori(0, FT // 2) as it:
                    for j in range(2):
                        i0 = FT * half + j
                        pool.wait_ge(w2_in[j], it * 16 + 16 * (FT // 2 * half + 1))
                        pool.wait_ge(ah_used, it * 2 + (i0 + 1))
                        take_wait()
                        pool.tensor_copy(w2_hl[0][:, j], w2raw[:, j]).then_inc(w2_hi_ok, 1)
                        pool.wait_ge(w2_hi_ok, it * 2 + (i0 + 1))
                        pool.tensor_tensor(w2_hl[1][:, j], w2raw[:, j], w2_hl[0][:, j].bitcast(F32), ALU.subtract)\
                            .then_inc(w2_split, 1)

        @block.scalar
        def _(act):
            def norm_rows(half):
                act.wait_ge(x_in[half], 64)
                for t in range(4 * half, 4 * half + 4):
                    nc.scalar.activation(junk[:, :], xin[:, t], ACT.Square, accum_out=ssq[:, t:t + 1]).then_inc(ssq_ok, 1)
                    act.wait_ge(ssq_ok, t + 1)
                act.wait_ge(var_ok, half + 1)
                nc.scalar.activation(rms[:, 4 * half:4 * half + 4], var[:, 4 * half:4 * half + 4], ACT.Sqrt)\
                    .then_inc(rms_ok, 1)
                act.wait_ge(rstd_ok, half + 1)
                for t in range(4 * half, 4 * half + 4):
                    ins = nc.scalar.activation(xin[:, t], xin[:, t], ACT.Copy, scale=rstd[:, t:t + 1])
                ins.then_inc(xn_ok, 1)

            def h_hi_part(g, scale, shift):
                act.wait_ge(xt_ready, g + 1)
                k, half = g % KD, g // KD % 2
                nc.scalar.activation(act_hl[0][:, k, half * NT:(half + 1) * NT], PS[:, h_bank(g)], ACT.Identity,
                                     bias=shift[:, k:k + 1], scale=scale[:, k:k + 1]).then_inc(h_hi, 1)

            def v_hi_part(t):
                act.wait_ge(v_ready, 2 * t + 1)
                nc.scalar.activation(va_hl[:, t, :, 0, :], PS[:, 7, B_H:B_H + VA_W].rearrange("p (h d) -> p h d", h=A_KV),
                                     ACT.Copy).then_inc(v_hi_ok, 1)
                act.wait_ge(v_ready, 2 * t + 2)
                nc.scalar.activation(vb_hl[:, t, :, 0, :], PS[:, 5 + t % 2, 0:VB_W].rearrange("p (h d) -> p h d", h=B_H),
                                     ACT.Copy).then_inc(v_hi_ok, 1)

            norm_rows(0)
            act.wait_ge(ada_taken, 1)
            for g in range(KD):
                h_hi_part(g, a_mix, adac)
                act.wait_ge(wv_in[g], 32)
                nc.scalar.activation(wv_hl[0][:, g], wvraw[:, g], ACT.Copy).then_inc(wv_hi_ok, 1)
            norm_rows(1)
            v_hi_part(0)
            for t in range(2):
                for g in range(KD + 4 * t, KD + 4 * t + 4):
                    h_hi_part(g, a_mix, adac)
                v_hi_part(t + 1)
            act.wait_ge(const_ok, 1)
            act.wait_ge(reduced, 2)
            nc.scalar.activation(cs[:, 0, 0], cs[:, 0, 0], ACT.Sin).then_inc(tables, 1)
            nc.scalar.activation(cs[:, 0, 1], cs[:, 0, 1], ACT.Sin, scale=sgn[:, 0:1]).then_inc(tables, 1)
            for t in range(3, NTOK):
                v_hi_part(t)

            def exps(u):
                w = width(u) + (u < 64)
                act.wait_ge(s_taken, u + 1)
                if u >= 8:
                    act.wait_ge(rden_ok, (u - 8) // 2 + 1)
                probs = scores_slot(u)[:, 0:w]
                nc.scalar.activation(probs, probs, ACT.Exp, bias=nmax[:, u % 8:u % 8 + 1],
                                     scale=-1.0, accum_out=den[:, u % 8:u % 8 + 1]).then_inc(p_ready, 1)

            def group_hi(g, slot, n):
                act.wait_ge(grp_ready, g + 1)
                if slot >= 4:
                    act.wait_ge(pv_done, slot - 3)
                nc.scalar.activation(pt_hl[0][:, slot % 4, 0:n], PS[:, 5 + g % 2, 0:n], ACT.Copy).then_inc(grp_hi, 1)

            def out_tile(tile):
                g = o_group[tile]
                act.wait_ge(grp_ready, g + 1)
                if tile >= 4:
                    act.wait_ge(o_out[tile % 4], 16 * (tile // 4))
                nc.scalar.activation(ostage[:, tile % 4], PS[:, 5 + g % 2, 0:P], ACT.Copy).then_inc(grp_hi, 1)
                return g

            def send_tile(tile):
                act.wait_ge(grp_hi, o_group[tile] + 1)
                p, i = tile // NTOK, tile % NTOK
                act.dma_start(oT_dram[p, :, i * P:(i + 1) * P], ostage[:, tile % 4]).then_inc(o_out[tile % 4], 16)

            exps(0)
            act.wait_ge(absz_ok, 1)
            nc.scalar.activation(ez[:, :, :], absz[:, :, :], ACT.Exp, scale=-1.0).then_inc(ez_ok, 1)
            act.wait_ge(onep_ok, 1)
            nc.scalar.activation(lnp[:, :, :], onep[:, :, :], ACT.Ln).then_inc(lnp_ok, 1)
            for u in range(NU + 3):
                if u + 1 < NU:
                    exps(u + 1)
                if u < NU:
                    for g, slot, blocks in p_groups[u]:
                        group_hi(g, slot, P * len(blocks))
                if u % 2 == 0 and u >= 4:
                    out_tile((u - 4) // 2)
                    send_tile((u - 4) // 2)
                for j, _ in evac_at[u] if u < NU else ():
                    if chunks[j][4] == "plain":
                        _, ch, dst, slot, _ = chunks[j]
                        act.wait_ge(proj_ready, j + 1)
                        nc.scalar.activation(dst[0][:, slot, ch * NT:(ch + 1) * NT], PS[:, chunk_bank[j]], ACT.Copy).then_inc(proj_hi, 1)

            act.wait_ge(pv_done, np_groups)
            for i in range(4):
                act.wait_ge(o_out[i], 16 * (PAIRS * NTOK // 4))
            for p in range(8):
                act.dma_start(merged[:, p, :], oT_dram[p]).then_inc(ob_in, 16)

            def gate(m4, m2, j):
                act.wait_ge(g_ready, m4 + (j + 5))
                act.wait_ge(merged_ok, m2 + (j % 2 + 1))
                nc.scalar.activation(sg[:, j], PS[:, j], ACT.Sigmoid).then_inc(g_done, 1)

            def outputs_hi(p):
                nc.scalar.activation(ob_hl[0][:, p], merged[:, p], ACT.Copy).then_inc(ob_hi_ok, 1)

            act.wait_ge(ob_in, 16 * 8)
            for p in range(8):
                outputs_hi(p)
            with act.Fori(0, KD // 2) as it:
                for mm in range(2):
                    for j in range(4):
                        gate(it * 8 + 4 * mm, it * 4 + 2 * mm, j)

            def merged_hi(k, half):
                cols = slice(half * NT, (half + 1) * NT)
                nc.scalar.activation(act_hl[0][:, k, cols], merged[:, k, cols], ACT.Copy).then_inc(m_hi_ok, 1)

            act.wait_ge(br_ready, 4 + 4 * KD)
            act.wait_ge(merged_ok, 2 + 2 * KD)
            for k in range(KD):
                act.wait_ge(wo_in[k % 2], 16 * (k // 2 + 1))
                nc.scalar.activation(ob_hl[0][:, k], woraw[:, k % 2], ACT.Copy).then_inc(wo_hi_ok, 1)
                merged_hi(k, 0)
            for k in range(KD):
                merged_hi(k, 1)
            for i in range(2):
                for hb in range(2):
                    act.wait_ge(grow_ready, 2 * i + hb + 1)
                    nc.scalar.activation(grow[:, i, hb * NT:(hb + 1) * NT], PS[:, 6 + hb], ACT.Copy).then_inc(grow_ok, 1)

            def y_squares(t):
                b = y_bank(t)
                act.wait_ge(y_ready, t + 1)
                if t > 0:
                    act.wait_ge(y_sq, t)
                else:
                    act.wait_ge(m_split, 2 * KD)
                nc.scalar.activation(junk2[:, :], PS[:, b:b + 2].rearrange("p a n -> p (a n)"), ACT.Square,
                                     accum_out=ssq[:, 8 + t:9 + t]).then_inc(y_sq, 1)
                act.wait_ge(y_var, t + 1)
                nc.scalar.activation(rms[:, 8 + t:9 + t], var[:, 8 + t:9 + t], ACT.Sqrt).then_inc(y_rms, 1)

            def x1_squares(t):
                act.wait_ge(x1_ok, t + 1)
                if t > 0:
                    act.wait_ge(x1_sq, t)
                nc.scalar.activation(junk_x[:, :], x1[:, t % 2], ACT.Square, accum_out=ssq[:, 16 + t:17 + t])\
                    .then_inc(x1_sq, 1)
                act.wait_ge(x1_var, t + 1)
                nc.scalar.activation(rms[:, 16 + t:17 + t], var[:, 16 + t:17 + t], ACT.Sqrt).then_inc(x1_rms, 1)

            for kind, t in MIX_ORDER:
                if kind == "residual":
                    y_squares(t)
                elif kind == "norm":
                    x1_squares(t)
                else:
                    for k in range(KD):
                        h_hi_part(KD * (2 + t) + k, a_ffn, adac[:, 3 * KD:4 * KD])

            def silu(ff, ch):
                nc.scalar.activation(sl[:, 2 * ff + ch], PS[:, 4 * (1 - ff) + ch], ACT.Silu).then_inc(silu_ok, 1)

            for ff in range(2):
                for ch in range(CH):
                    act.wait_ge(ff_ready, (1, 3, 5, 6)[2 * ff + ch])
                    silu(ff, ch)
            with act.Fori(1, FT // 2) as it:
                for ff in range(2):
                    for ch in range(CH):
                        act.wait_ge(ff_ready, it * 8 + (4 * ff + ch + 1))
                        act.wait_ge(ff_ok, it * 4 + (2 * ff + ch + 1))
                        silu(ff, ch)
            act.wait_ge(ff_ready, 4 * FT)
            act.wait_ge(ff_ok, 4 + 2 * FT)
            for half in range(2):
                with act.Fori(0, FT // 2) as it:
                    for j in range(2):
                        act.wait_ge(ah_used, it * 2 + (FT * half + j + 1))
                        nc.scalar.activation(ah_hl[0][:, j], act_ff[:, bass.ds(it * 2 + j, 1), :]
                                             .rearrange("p a n -> p (a n)"), ACT.Copy).then_inc(ah_hi_ok, 1)
                if half == 0:
                    for t in range(NTOK):
                        act.wait_ge(z_taken, t + 1)
                        if t > 0:
                            act.wait_ge(z_sq, t)
                        nc.scalar.activation(junk3[:, 0:NT], y0[:, t], ACT.Square, accum_out=ssq[:, 24 + t:25 + t])\
                            .then_inc(z_sq, 1)
            for t in range(NTOK):
                act.wait_ge(z_ready, NTOK + t + 1)
                act.wait_ge(z_sq, NTOK + t)
                nc.scalar.activation(junk3[:, 0:NT], PS[:, t], ACT.Square, accum_out=ssq_b[:, t:t + 1]).then_inc(z_sq, 1)
                act.wait_ge(z_var, t + 1)
                nc.scalar.activation(rms[:, 24 + t:25 + t], var[:, 24 + t:25 + t], ACT.Sqrt).then_inc(z_rms, 1)

        @block.vector
        def _(dve):
            step = [0]

            def link(ins):
                step[0] += 1
                ins.then_inc(dve_step, 1)
                dve.wait_ge(dve_step, step[0])

            nc.vector.memset(credit[:, 0:1], 0.0).then_inc(merged_ok, 2)
            nc.vector.memset(credit[:, 1:2], 0.0).then_inc(ff_ok, 4)
            nc.vector.memset(credit[:, 2:3], 0.0).then_inc(br_taken, 4)
            nc.vector.memset(credit[:, 3:4], 0.0).then_inc(ah_used, 2)
            nc.vector.memset(credit[:, 4:5], 0.0).then_inc(w2_split, 2)
            nc.vector.memset(credit[:, 5:6], 0.0).then_inc(g_ready, 4)
            nc.vector.memset(credit[:, 6:7], 0.0).then_inc(br_ready, 4)
            nc.vector.memset(credit[:, 7:8], 0.0).then_inc(g_done, 4)

            def norm_rows(half):
                cols = slice(4 * half, 4 * half + 4)
                dve.wait_ge(ssq_ok, 4 * half + 4)
                nc.vector.tensor_scalar(var[:, cols], ssq[:, cols], 1.0 / D, EPS, ALU.mult, ALU.add).then_inc(var_ok, 1)
                dve.wait_ge(rms_ok, half + 1)
                nc.vector.reciprocal(rstd[:, cols], rms[:, cols]).then_inc(rstd_ok, 1)

            dve.wait_ge(bc_in, 64)
            link(nc.vector.tensor_scalar(nsink[:, :], sinkb[:, :], -1.0, None, ALU.mult))
            dve.wait_ge(prow_ready, 1)
            nc.vector.tensor_copy(pcols[:, :], PS[:, 5, 0:88]).then_inc(pcols_ok, 1)
            dve.wait_ge(pcols_ok, 1)
            for j in range(4):
                dve.wait_ge(ada_in[j % 2], 16 * (j // 2 + 1))
                if j >= 2:
                    dve.wait_ge(ada_used, j - 1)
                acc = ada_acc[:, j % 2]
                link(nc.vector.tensor_scalar(acc, wada[:, j % 2, 0], pcols[:, 0:1], None, ALU.mult))
                for k in range(1, KD):
                    ins = nc.vector.scalar_tensor_tensor(out=acc, in0=wada[:, j % 2, k], scalar=pcols[:, k:k + 1], in1=acc,
                                                         op0=ALU.mult, op1=ALU.add)
                    if k < KD - 1:
                        link(ins)
                ins.then_inc(acc_ready, 1)
                if j == 0:
                    norm_rows(0)
            dve.wait_ge(ada_used, 4)
            link(nc.vector.tensor_tensor(adac[:, 0:2 * KD], PS[:, 4, 0:2 * KD], pcols[:, KD:3 * KD], ALU.add))
            nc.vector.scalar_tensor_tensor(out=a_mix[:, :], in0=adac[:, KD:2 * KD], scalar=1.0,
                                           in1=pcols[:, 7 * KD:8 * KD], op0=ALU.add, op1=ALU.mult).then_inc(ada_taken, 1)
            dve.wait_ge(ada_taken, 1)

            def h_lo_part(g, scale, shift, tmp):
                k, half = g % KD, g // KD % 2
                dve.wait_ge(h_hi, g + 1)
                nc.vector.tensor_scalar(tmp[:, g % 2], PS[:, h_bank(g)], scale[:, k:k + 1], shift[:, k:k + 1],
                                        ALU.mult, ALU.add).then_inc(h_tmp, 1)
                dve.wait_ge(h_tmp, g + 1)
                cols = slice(half * NT, (half + 1) * NT)
                nc.vector.tensor_tensor(act_hl[1][:, k, cols], tmp[:, g % 2], act_hl[0][:, k, cols].bitcast(F32),
                                        ALU.subtract).then_inc(h_lo, 1)

            def v_lo_part(t):
                dve.wait_ge(v_hi_ok, 2 * t + 1)
                if t == 0:
                    dve.wait_ge(bc_in, 64)
                nc.vector.tensor_tensor(z[:, t], PS[:, 7, 0:B_H], bfb[:, :], ALU.add)
                nc.vector.tensor_tensor(va_hl[:, t, :, 1, :], PS[:, 7, B_H:B_H + VA_W].rearrange("p (h d) -> p h d", h=A_KV),
                                        va_hl[:, t, :, 0, :].bitcast(F32), ALU.subtract).then_inc(v_taken, 1)
                dve.wait_ge(v_hi_ok, 2 * t + 2)
                nc.vector.tensor_tensor(vb_hl[:, t, :, 1, :], PS[:, 5 + t % 2, 0:VB_W].rearrange("p (h d) -> p h d", h=B_H),
                                        vb_hl[:, t, :, 0, :].bitcast(F32), ALU.subtract).then_inc(v_taken, 1)

            for g in range(KD):
                h_lo_part(g, a_mix, adac, htmp)
            norm_rows(1)
            v_lo_part(0)
            for t in range(2):
                for g in range(KD + 4 * t, KD + 4 * t + 4):
                    h_lo_part(g, a_mix, adac, htmp)
                v_lo_part(t + 1)
            def rope_products(j, bank, part):
                ch = chunks[j][1]
                cols = slice(ch * NT, (ch + 1) * NT)
                if part == 0:
                    dve.wait_ge(proj_ready, j + 1)
                    if j == 0:
                        dve.wait_ge(tables, 2)
                    else:
                        dve.wait_ge(rope_done, j)
                    nc.vector.tensor_tensor(rope_a[:, :], PS[:, bank], cs[:, 0, 0, cols], ALU.mult)
                for quad in ((), (0, 1), (2,), (3,))[part]:
                    o, i = 32 * quad, 32 * (quad ^ 1)
                    ins = nc.vector.tensor_tensor(rope_b[o:o + 32, :], PS[i:i + 32, bank], cs[i:i + 32, 0, 1, cols], ALU.mult)
                if part == 3:
                    ins.then_inc(proj_taken, 1)

            dve.wait_ge(bc_in, 64)
            link(nc.vector.tensor_copy(ang[:, :], posi[:, :]))
            link(nc.vector.tensor_scalar(ang[:, :], ang[:, :], invf[:, 0:1], None, ALU.mult))
            for which, quarter in ((0, 0.25), (1, 0.0)):
                r = cs[:, 0, which]
                link(nc.vector.tensor_scalar(turns[:, :], ang[:, :], 1.0 / (2 * math.pi), quarter, ALU.mult, ALU.add))
                link(nc.vector.tensor_scalar(turns[:, :], turns[:, :], ROUND, ROUND, ALU.add, ALU.subtract))
                link(nc.vector.scalar_tensor_tensor(out=r, in0=turns[:, :], scalar=-TURN[0], in1=ang[:, :],
                                                    op0=ALU.mult, op1=ALU.add))
                for part in TURN[1:]:
                    link(nc.vector.scalar_tensor_tensor(out=r, in0=turns[:, :], scalar=-part, in1=r,
                                                        op0=ALU.mult, op1=ALU.add))
                link(nc.vector.tensor_scalar(r, r, 2 * math.pi * quarter, PI_BELOW, ALU.add, ALU.min))
                nc.vector.tensor_scalar(r, r, -PI_BELOW, None, ALU.max).then_inc(reduced, 1)

            v_lo_part(3)
            for t in range(4, NTOK):
                for part in range(4):
                    rope_products(t - 4, t - 4, part)
                v_lo_part(t)

            def max_and_scale(u):
                p, i, h = parts(u)
                w = width(u)
                dve.wait_ge(s_ready, u + 1)
                if u >= 3:
                    dve.wait_ge(grp_ready, p_groups[u - 3][-1][0] + 1)
                src = PS[:, 1 + 2 * (u % 2):3 + 2 * (u % 2)].rearrange("p a n -> p (a n)")[:, 0:w]
                if p < 4:
                    sink = nsink[:, p + 4 * h:p + 4 * h + 1]
                    bias, least = band[:, 2 * P - w:2 * P], sink
                    nc.vector.tensor_copy(scores_slot(u)[:, w:w + 1], sink)
                else:
                    slot = 1 - p % 2
                    if i == 0 and h == 0:
                        dve.wait_ge(cum_in[slot], 16 * ((p - 4) // 2 + 1))
                    bias, least = cs[:, slot, h, 0:w], BIG
                nc.vector.tensor_tensor_reduce(out=scores_slot(u)[:, 0:w], in0=src, in1=bias, scale=-SM, scalar=least,
                                               op0=ALU.add, op1=ALU.min, accum_out=nmax[:, u % 8:u % 8 + 1])\
                    .then_inc(s_taken, 1)

            def group_lo(g, slot, n):
                dve.wait_ge(grp_hi, g + 1)
                nc.vector.tensor_tensor(pt_hl[1][:, slot % 4, 0:n], PS[:, 5 + g % 2, 0:n],
                                        pt_hl[0][:, slot % 4, 0:n].bitcast(F32), ALU.subtract).then_inc(grp_lo, 1)

            def normalise(tile):
                u = 2 * tile
                dve.wait_ge(pv_done, p_groups[u + 1][-1][1] + 1)
                nc.vector.reciprocal(rden[:, tile % 2], den[:, u % 8:u % 8 + 2]).then_inc(rden_ok, 1)
                if tile >= 2:
                    dve.wait_ge(grp_ready, o_group[tile - 2] + 1)
                sums = PS[:, 7, 0:2 * P].rearrange("p (h a d) -> p h a d", h=2, a=2)
                link(nc.vector.tensor_copy(ot[:, tile % 2], sums[:, :, 1]))
                nc.vector.tensor_tensor(ot[:, tile % 2], sums[:, :, 0], ot[:, tile % 2], ALU.add).then_inc(o_taken, 1)
                dve.wait_ge(o_taken, tile + 1)
                dve.wait_ge(rden_ok, tile + 1)
                nc.vector.tensor_tensor(o_sb[:, tile % 2].rearrange("p (h d) -> p h d", h=2), ot[:, tile % 2],
                                        rden[:, tile % 2].unsqueeze(2).broadcast_to([P, 2, HALF]), ALU.mult)\
                    .then_inc(o_ok, 1)

            max_and_scale(0)
            max_and_scale(1)
            dve.wait_ge(v_taken, 2 * NTOK)
            nc.vector.scalar_tensor_tensor(out=absz[:, :, :], in0=z[:, :, :], scalar=-1.0, in1=z[:, :, :],
                                           op0=ALU.mult, op1=ALU.max).then_inc(absz_ok, 1)
            dve.wait_ge(ez_ok, 1)
            nc.vector.tensor_scalar(onep[:, :, :], ez[:, :, :], 1.0, None, ALU.add).then_inc(onep_ok, 1)
            dve.wait_ge(onep_ok, 1)
            link(nc.vector.scalar_tensor_tensor(out=corr[:, :, :], in0=onep[:, :, :], scalar=-1.0, in1=ez[:, :, :],
                                                op0=ALU.add, op1=ALU.subtract))
            dve.wait_ge(lnp_ok, 1)
            link(nc.vector.tensor_tensor(lnp[:, :, :], lnp[:, :, :], corr[:, :, :], ALU.subtract))
            link(nc.vector.scalar_tensor_tensor(out=nlf[:, :, :], in0=z[:, :, :], scalar=0.0, in1=lnp[:, :, :],
                                                op0=ALU.min, op1=ALU.subtract))
            link(nc.vector.tensor_scalar(nlf[:, :, :], nlf[:, :, :], -1.0, None, ALU.mult))
            link(nc.vector.memset(pref[:, 0], 0.0))
            for t in range(1, NTOK):
                ins = nc.vector.tensor_tensor(pref[:, t], pref[:, t - 1], nlf[:, t - 1], ALU.add)
                if t < NTOK - 1:
                    link(ins)
                else:
                    ins.then_inc(nlf_ok, 1)

            for u in range(NU + 2):
                if u >= 3 and u % 2 == 1:
                    normalise((u - 3) // 2)
                if u + 2 < NU:
                    max_and_scale(u + 2)
                if u < NU:
                    for g, slot, blocks in p_groups[u]:
                        group_lo(g, slot, P * len(blocks))
                if CUM_STEP <= u < CUM_STEP + CH:
                    cc = u - CUM_STEP
                    dve.wait_ge(cum_ready, cc + 1)
                    nc.vector.tensor_scalar(ncum[:, cc * NT:(cc + 1) * NT], PS[0:B_H, 0, :], 1.0 / SM, None, ALU.mult)\
                        .then_inc(cum_taken, 1)
                for j, part in evac_at[u] if u < NU else ():
                    _, ch, dst, slot, kind = chunks[j]
                    cols = slice(ch * NT, (ch + 1) * NT)
                    if kind == "rope":
                        rope_products(j, chunk_bank[j], part)
                    else:
                        dve.wait_ge(proj_hi, j - N_ROPE + 1)
                        nc.vector.tensor_tensor(dst[1][:, slot, cols], PS[:, chunk_bank[j]], dst[0][:, slot, cols].bitcast(F32),
                                                ALU.subtract).then_inc(proj_taken, 1)

            for p in range(8):
                dve.wait_ge(ob_hi_ok, p + 1)
                nc.vector.tensor_tensor(ob_hl[1][:, p], merged[:, p], ob_hl[0][:, p].bitcast(F32), ALU.subtract)\
                    .then_inc(ob_split, 1)
            with dve.Fori(0, KD // 2) as it:
                for mm in range(2):
                    for j in range(4):
                        a = 4 * mm + j
                        dve.wait_ge(ada2_in[a % 2], it * 64 + 16 * (a // 2 + 1))
                        nc.vector.tensor_tensor(adaraw[:, a % 2], adaraw[:, a % 2],
                                                pcols[:, 0:KD].unsqueeze(2).broadcast_to([P, KD, P]), ALU.mult)\
                            .then_inc(ada_prod, 1)
                        dve.wait_ge(ada_prod, it * 8 + (a + 1))
                        dve.wait_ge(ada_used, it * 8 + (a + 3))
                        nc.vector.tensor_reduce(out=ada_acc2[:, a % 2], in_=adaraw[:, a % 2].rearrange("p k n -> p n k"),
                                                op=ALU.add, axis=mybir.AxisListType.X).then_inc(acc_ready, 1)
                    for j in range(4):
                        dve.wait_ge(g_done, it * 8 + (4 * mm + j + 5))
                        dve.wait_ge(br_ready, it * 8 + (4 * mm + j + 5))
                        nc.vector.tensor_tensor(sg[:, j], PS[:, BR_BANK[j]], sg[:, j], ALU.mult).then_inc(br_taken, 1)
                    for ch in range(CH):
                        dve.wait_ge(br_taken, it * 8 + (4 * mm + ch + 7))
                        nc.vector.tensor_tensor(merged[:, bass.ds(it * 2 + mm, 1), ch * NT:(ch + 1) * NT]
                                                .rearrange("p a n -> p (a n)"), sg[:, ch], sg[:, 2 + ch], ALU.add)\
                            .then_inc(merged_ok, 1)

            def merged_lo(k, half):
                cols = slice(half * NT, (half + 1) * NT)
                dve.wait_ge(m_hi_ok, half * KD + k + 1)
                nc.vector.tensor_tensor(act_hl[1][:, k, cols], merged[:, k, cols], act_hl[0][:, k, cols].bitcast(F32),
                                        ALU.subtract).then_inc(m_split, 1)

            dve.wait_ge(merged_ok, 2 + 2 * KD)
            for k in range(KD):
                dve.wait_ge(wo_hi_ok, k + 1)
                nc.vector.tensor_tensor(ob_hl[1][:, k], woraw[:, k % 2], ob_hl[0][:, k].bitcast(F32), ALU.subtract)\
                    .then_inc(wo_split, 1)
                merged_lo(k, 0)
            dve.wait_ge(ada_used, 4 + N_ADA)
            link(nc.vector.tensor_tensor(adac[:, 2 * KD:6 * KD], PS[:, 7, 0:N_ADA], pcols[:, 3 * KD:7 * KD], ALU.add))
            nc.vector.tensor_tensor(gm_col[:, 0:KD], adac[:, 2 * KD:3 * KD], pcols[:, 8 * KD:9 * KD], ALU.mult)
            nc.vector.tensor_tensor(gm_col[:, KD:2 * KD], adac[:, 5 * KD:6 * KD], pcols[:, 10 * KD:11 * KD], ALU.mult)
            link(nc.vector.scalar_tensor_tensor(out=a_ffn[:, :], in0=adac[:, 4 * KD:5 * KD], scalar=1.0,
                                                in1=pcols[:, 9 * KD:10 * KD], op0=ALU.add, op1=ALU.mult))
            for r in range(4):
                if r > 0:
                    dve.wait_ge(grow_ready, r)
                for kk in range(4):
                    ins = nc.vector.tensor_scalar(diag[:, kk], ident[:, :], gm_col[:, 4 * r + kk:4 * r + kk + 1], None, ALU.mult)
                ins.then_inc(diag_ok, 1)
            for k in range(KD):
                merged_lo(k, 1)

            def residual(t):
                b = y_bank(t)
                dve.wait_ge(y_sq, t + 1)
                nc.vector.tensor_scalar(var[:, 8 + t:9 + t], ssq[:, 8 + t:9 + t], 1.0 / D, EPS, ALU.mult, ALU.add).then_inc(y_var, 1)
                dve.wait_ge(y_rms, t + 1)
                link(nc.vector.reciprocal(rstd[:, 8 + t:9 + t], rms[:, 8 + t:9 + t]))
                if t == 0:
                    dve.wait_ge(grow_ok, 4)
                if t >= 2:
                    dve.wait_ge(x1_out[t % 2], 16 * (t // 2))
                    dve.wait_ge(xn_ok, 2 + t - 1)
                nc.vector.scalar_tensor_tensor(out=x1[:, t % 2], in0=PS[:, b:b + 2].rearrange("p a n -> p (a n)"),
                                               scalar=rstd[:, 8 + t:9 + t], in1=grow[:, 0], op0=ALU.mult,
                                               op1=ALU.mult).then_inc(y_taken, 1)
                dve.wait_ge(y_taken, t + 1)
                dve.wait_ge(xr_in[t % 2], 16 * (t // 2 + 1))
                nc.vector.tensor_tensor(x1[:, t % 2], x1[:, t % 2], xr[:, t % 2], ALU.add).then_inc(x1_ok, 1)

            def x1_norm(t):
                dve.wait_ge(x1_sq, t + 1)
                nc.vector.tensor_scalar(var[:, 16 + t:17 + t], ssq[:, 16 + t:17 + t], 1.0 / D, EPS, ALU.mult, ALU.add).then_inc(x1_var, 1)
                dve.wait_ge(x1_rms, t + 1)
                link(nc.vector.reciprocal(rstd[:, 16 + t:17 + t], rms[:, 16 + t:17 + t]))
                if t >= 4:
                    dve.wait_ge(xt_ready, 3 * KD)
                nc.vector.tensor_scalar(xn[:, t % 4], x1[:, t % 2], rstd[:, 16 + t:17 + t], None, ALU.mult).then_inc(xn_ok, 1)

            def h_tmp_part(g):
                k = g % KD
                dve.wait_ge(h_hi, g + 1)
                if g >= 2 * KD + 2:
                    dve.wait_ge(h_lo, g - 1)
                nc.vector.tensor_scalar(htmp2[:, g % 2], PS[:, h_bank(g)], a_ffn[:, k:k + 1], adac[:, 3 * KD + k:3 * KD + k + 1],
                                        ALU.mult, ALU.add).then_inc(h_tmp, 1)

            for kind, t in MIX_ORDER:
                if kind == "residual":
                    residual(t)
                elif kind == "norm":
                    x1_norm(t)
                else:
                    for k in range(KD):
                        h_tmp_part(KD * (2 + t) + k)

            for ff in range(2):
                for ch in range(CH):
                    dve.wait_ge(silu_ok, 2 * ff + ch + 1)
                    dve.wait_ge(ff_ready, (2, 4, 7, 8)[2 * ff + ch])
                    nc.vector.tensor_tensor(act_ff[:, ff, ch * NT:(ch + 1) * NT], PS[:, 4 * (1 - ff) + 2 + ch],
                                            sl[:, 2 * ff + ch], ALU.mult).then_inc(ff_ok, 1)
            with dve.Fori(1, FT // 2) as it:
                for ff in range(2):
                    for ch in range(CH):
                        dve.wait_ge(silu_ok, it * 4 + (2 * ff + ch + 1))
                        dve.wait_ge(ff_ready, it * 8 + (4 * ff + 2 + ch + 1))
                        nc.vector.tensor_tensor(act_ff[:, bass.ds(it * 2 + ff, 1), ch * NT:(ch + 1) * NT]
                                                .rearrange("p a n -> p (a n)"), PS[:, 4 * (1 - ff) + 2 + ch],
                                                sl[:, 2 * ff + ch], ALU.mult).then_inc(ff_ok, 1)
            for half in range(2):
                with dve.Fori(0, FT // 2) as it:
                    for j in range(2):
                        dve.wait_ge(ah_hi_ok, it * 2 + (FT * half + j + 1))
                        nc.vector.tensor_tensor(ah_hl[1][:, j], act_ff[:, bass.ds(it * 2 + j, 1), :]
                                                .rearrange("p a n -> p (a n)"), ah_hl[0][:, j].bitcast(F32),
                                                ALU.subtract).then_inc(ah_split, 1)
                if half == 0:
                    for t in range(NTOK):
                        dve.wait_ge(z_ready, t + 1)
                        nc.vector.tensor_copy(y0[:, t], PS[:, t]).then_inc(z_taken, 1)
            for t in range(NTOK):
                dve.wait_ge(z_sq, NTOK + t + 1)
                link(nc.vector.tensor_tensor(ssq[:, 24 + t:25 + t], ssq[:, 24 + t:25 + t], ssq_b[:, t:t + 1], ALU.add))
                nc.vector.tensor_scalar(var[:, 24 + t:25 + t], ssq[:, 24 + t:25 + t], 1.0 / D, EPS, ALU.mult, ALU.add).then_inc(z_var, 1)
                dve.wait_ge(z_rms, t + 1)
                link(nc.vector.reciprocal(rstd[:, 24 + t:25 + t], rms[:, 24 + t:25 + t]))
                if t >= 2:
                    dve.wait_ge(done[t % 2], 16 * (t // 2))
                dve.wait_ge(x1r_in[t % 4], 16 * (t // 4 + 1))
                for hb, y in ((0, y0[:, t]), (1, PS[:, t])):
                    ins = nc.vector.scalar_tensor_tensor(out=fin[:, t % 2, hb * NT:(hb + 1) * NT], in0=y,
                                                         scalar=rstd[:, 24 + t:25 + t],
                                                         in1=grow[:, 1, hb * NT:(hb + 1) * NT], op0=ALU.mult, op1=ALU.mult)
                link(ins)
                nc.vector.tensor_tensor(fin[:, t % 2], fin[:, t % 2], x1r[:, t % 4], ALU.add).then_inc(fin_ok, 1)

        @block.tensor
        def _(pe):
            def product(out_ap, lhs, rhs, first, last):
                for i, (a, b) in enumerate(TERMS):
                    ins = nc.tensor.matmul(out_ap, lhs[a], rhs[b], start=first and i == 0, stop=last and i == 2)
                return ins

            def transpose_group(g, src):
                k = g % KD
                if 4 <= g < 2 * KD:
                    pe.wait_ge(h_tmp, g - 3)
                elif g >= 2 * KD + 2:
                    pe.wait_ge(h_tmp, g - 1)
                for tt in range(4):
                    ins = nc.tensor.transpose(PS[:, h_bank(g), tt * P:(tt + 1) * P], src[:, tt, k * P:(k + 1) * P], ident[:, :])
                ins.then_inc(xt_ready, 1)

            pe.wait_ge(par_in, 96)
            pe.wait_ge(const_ok, 1)
            nc.tensor.transpose(PS[:, 5, 0:88], prow[:, :], ident[0:88, 0:88]).then_inc(prow_ready, 1)
            pe.wait_ge(xn_ok, 1)
            for g in range(4):
                transpose_group(g, xin[:, 0:4])
            for j in range(4):
                pe.wait_ge(acc_ready, j + 1)
                for oc in range(4):
                    ins = nc.tensor.matmul(PS[:, 4, 4 * j + oc:4 * j + oc + 1], ada_acc[:, j % 2, oc * P:(oc + 1) * P],
                                           ones[:, 0:1], start=True, stop=True)
                ins.then_inc(ada_used, 1)
            for g in range(4, KD):
                transpose_group(g, xin[:, 0:4])

            def values(t):
                cols = slice(t * P, (t + 1) * P)
                pe.wait_ge(h_lo, KD * (1 + t // 4))
                if t == 0:
                    pe.wait_ge(wv_split, KD)
                else:
                    pe.wait_ge(v_taken, 2 * t - 1)
                for k in range(KD):
                    ins = product(PS[:, 7, 0:B_H + VA_W], [a[:, k, cols] for a in act_hl],
                                  [w[:, k, VB_W:WV] for w in wv_hl], k == 0, k == KD - 1)
                ins.then_inc(v_ready, 1)
                if t >= 2:
                    pe.wait_ge(v_taken, 2 * t - 2)
                for k in range(KD):
                    ins = product(PS[:, 5 + t % 2], [a[:, k, cols] for a in act_hl],
                                  [w[:, k, 0:VB_W] for w in wv_hl], k == 0, k == KD - 1)
                ins.then_inc(v_ready, 1)

            values(0)
            pe.wait_ge(xn_ok, 2)
            for t in range(2):
                for g in range(KD + 4 * t, KD + 4 * t + 4):
                    transpose_group(g, xin[:, 4:8])
                values(t + 1)
            def project(j, first, end):
                n, ch = chunks[j][:2]
                bank = chunk_bank[j]
                if first == 0:
                    pe.wait_ge(w_split, n + 1)
                    if j == 0:
                        pe.wait_ge(h_lo, 2 * KD)
                    elif bank == 0 and chunk_bank.index(0, 1) == j:
                        pe.wait_ge(cum_taken, CH)
                    elif j >= 4:
                        before = max(i for i in range(j) if chunk_bank[i] == bank)
                        pe.wait_ge(proj_taken, before + 1)
                for m in range(first, end):
                    k, (a, b) = m // 3, TERMS[m % 3]
                    ins = nc.tensor.matmul(PS[:, bank], w_hl[a][:, n % 2, k], act_hl[b][:, k, ch * NT:(ch + 1) * NT],
                                           start=(m == 0), stop=(m == 3 * KD - 1))
                if end == 3 * KD:
                    ins.then_inc(proj_ready, 1)

            for j in range(4):
                project(j, 0, 3 * KD)
            for t in range(3, NTOK):
                values(t)

            def cumulate(cc):
                if cc == 0:
                    pe.wait_ge(nlf_ok, 1)
                    pe.wait_ge(proj_taken, 1)
                else:
                    pe.wait_ge(cum_taken, cc)
                for tt in range(4):
                    t = 4 * cc + tt
                    dst = PS[0:B_H, 0, tt * P:(tt + 1) * P]
                    nc.tensor.matmul(dst, nlf[:, t], tri[:, :], start=True, stop=False)
                    ins = nc.tensor.matmul(dst, pref[:, t], ones[:, :], start=False, stop=True)
                ins.then_inc(cum_ready, 1)

            def scores(u):
                p, i, h = parts(u)
                if h == 0 and i % 4 == 0:
                    j = q_chunk[p][i // 4]
                    pe.wait_ge(rope_done if j < N_ROPE else proj_taken, j + 1)
                if p > 3 and i == 4 and h == 0 and p + 1 < PAIRS:
                    pe.wait_ge(proj_taken, q_chunk[p + 1][0] - 1)
                if u >= 2:
                    pe.wait_ge(s_taken, u - 1)
                else:
                    pe.wait_ge(proj_taken, 2 + 2 * u)
                rows = slice(h * HALF, (h + 1) * HALF)
                q = [a[rows, p % 2, i * P:(i + 1) * P] for a in q_hl]
                slot = 1 if p < 4 else p % 2
                k0, w = first_block(u) * P, width(u)
                for c0 in range(0, w, NT):
                    n = min(NT, w - c0)
                    dst = PS[:, 1 + 2 * (u % 2) + c0 // NT, 0:n]
                    keys = [a[rows, slot, k0 + c0:k0 + c0 + n] for a in k_hl]
                    for t, (a, b) in enumerate(TERMS):
                        ins = nc.tensor.matmul(dst, q[a], keys[b], start=(t == 0), stop=(t == 2))
                        if t == 0 and p >= 4 and c0 + n == w:
                            nc.tensor.matmul(dst[:, n - P:n], identb[:, :], causalb[:, :], start=False, stop=False)
                ins.then_inc(s_ready, 1)

            def free_bank(g):
                if g < 2:
                    pe.wait_ge(v_taken, 2 * NTOK)
                else:
                    kind, n = group_kind[g - 2]
                    pe.wait_ge(*((grp_lo, n + 1) if kind == "p" else (grp_hi, g - 1)))

            def transpose_p(u):
                pe.wait_ge(p_ready, u + 1)
                for g, slot, blocks in p_groups[u]:
                    free_bank(g)
                    for b in blocks:
                        ins = nc.tensor.transpose(PS[:, 5 + g % 2, (b - blocks[0]) * P:(b - blocks[0] + 1) * P],
                                                  scores_slot(u)[:, b * P:(b + 1) * P], ident[:, :])
                    ins.then_inc(grp_ready, 1)

            def times_v(u):
                p, i, h = parts(u)
                if h == 0:
                    if u == 0:
                        pe.wait_ge(v_taken, 2 * NTOK)
                    else:
                        pe.wait_ge(o_taken, u // 2)
                nb = width(u) // P
                for g, slot, blocks in p_groups[u]:
                    pe.wait_ge(grp_lo, slot + 1)
                    for b in blocks:
                        cols = slice((b - blocks[0]) * P, (b - blocks[0] + 1) * P)
                        whole, part = PS[:, 7, h * P:(h + 1) * P], PS[:, 7, h * P:h * P + HALF]
                        p_hi, p_lo = (a[:, slot % 4, cols] for a in pt_hl)
                        v_both, v_hi = (v_of(u, first_block(u) + b, lo) for lo in (False, True))
                        if nb == 1:
                            nc.tensor.matmul(whole, p_hi, v_both, start=True, stop=False)
                            ins = nc.tensor.matmul(whole, p_lo, v_both, start=False, stop=True)
                        elif b < nb - 1:
                            nc.tensor.matmul(whole, p_hi, v_both, start=(b == 0), stop=False)
                            ins = nc.tensor.matmul(part, p_lo, v_hi, start=False, stop=False)
                        else:
                            nc.tensor.matmul(part, p_lo, v_hi, start=False, stop=False)
                            ins = nc.tensor.matmul(whole, p_hi, v_both, start=False, stop=True)
                    ins.then_inc(pv_done, 1)

            scores(0)
            scores(1)
            for u in range(NU + 3):
                if u + 2 < NU:
                    scores(u + 2)
                if u < NU:
                    transpose_p(u)
                    if CUM_STEP <= u < CUM_STEP + CH:
                        cumulate(u - CUM_STEP)
                    for j, first, end in mm_at[u]:
                        project(j, first, end)
                if u % 2 == 0 and u >= 4:
                    tile = (u - 4) // 2
                    g = o_group[tile]
                    pe.wait_ge(o_ok, tile + 1)
                    free_bank(g)
                    nc.tensor.transpose(PS[:, 5 + g % 2, 0:P], o_sb[:, tile % 2], ident[:, :]).then_inc(grp_ready, 1)
                if 1 <= u <= NU:
                    times_v(u - 1)

            pe.wait_ge(proj_taken, len(chunks))
            pe.wait_ge(s_taken, NU)
            pe.wait_ge(o_taken, NU // 2)
            pe.wait_ge(grp_hi, len(group_kind))
            pe.wait_ge(grp_lo, np_groups)
            with pe.Fori(0, KD // 2) as it:
                for mm in range(2):
                    for r in range(3):
                        n = N_ATT + 3 * mm + r
                        pe.wait_ge(w_split, it * 6 + (n + 1))
                        if r < 2:
                            for ch in range(CH):
                                j = 2 * r + ch
                                if j < 3:
                                    pe.wait_ge(g_done, it * 8 + (4 * mm + j + 1))
                                else:
                                    pe.wait_ge(br_taken, it * 8 + (4 * mm + 4))
                                for k in range(KD):
                                    ins = product(PS[:, j], [w[:, n % 2, k] for w in w_hl],
                                                  [a[:, k, ch * NT:(ch + 1) * NT] for a in act_hl], k == 0, k == KD - 1)
                                ins.then_inc(g_ready, 1)
                        else:
                            pe.wait_ge(ob_split, 8)
                            for j in range(4):
                                ch = j % 2
                                if j < 3:
                                    pe.wait_ge(br_taken, it * 8 + (4 * mm + j + 1))
                                else:
                                    pe.wait_ge(g_done, it * 8 + (4 * mm + 8))
                                for kk in range(4):
                                    k = 4 * (j // 2) + kk
                                    ins = product(PS[:, BR_BANK[j]], [w[:, n % 2, k] for w in w_hl],
                                                  [a[:, k, ch * NT:(ch + 1) * NT] for a in ob_hl], kk == 0, kk == 3)
                                ins.then_inc(br_ready, 1)
                        for q in ((), (0, 1), (2, 3))[r]:
                            a = 4 * mm + q
                            pe.wait_ge(acc_ready, it * 8 + (a + 5))
                            nc.tensor.matmul(PS[:, 7, bass.ds(it * 8 + a, 1)], ada_acc2[:, a % 2], ones[:, 0:1],
                                             start=True, stop=True).then_inc(ada_used, 1)

            def out_proj(t, k):
                b = y_bank(t)
                for hb in range(2):
                    ins = product(PS[:, b + hb], [a[:, k, t * P:(t + 1) * P] for a in act_hl],
                                  [w[:, k, hb * NT:(hb + 1) * NT] for w in ob_hl], k == 0, k == KD - 1)
                if k == KD - 1:
                    ins.then_inc(y_ready, 1)

            pe.wait_ge(g_done, 4 + 4 * KD)
            pe.wait_ge(br_taken, 4 + 4 * KD)
            for k in range(KD):
                pe.wait_ge(wo_split, k + 1)
                pe.wait_ge(m_split, k + 1)
                for t in range(3):
                    out_proj(t, k)
                if k >= 4:
                    r = k - 4
                    pe.wait_ge(diag_ok, r + 1)
                    if r >= 2:
                        pe.wait_ge(grow_ok, r - 1)
                    nc.tensor.matmul(PS[:, 6 + r % 2], ones[:, :], diag[:, :, :].rearrange("p a n -> p (a n)"),
                                     start=True, stop=True).then_inc(grow_ready, 1)
            pe.wait_ge(m_split, 2 * KD)
            for t in range(3, NTOK):
                if t == 3:
                    pe.wait_ge(grow_ok, 4)
                else:
                    pe.wait_ge(y_taken, {4: 1, 5: 3, 6: 4, 7: 5}[t])
                if t == 5:
                    pe.wait_ge(y_taken, 2)
                for k in range(KD):
                    out_proj(t, k)
                    for kk in {(4, 6): (0,), (4, 7): (1,)}.get((t, k), (k + 2,) if t == 5 and k + 2 < KD else ()):
                        if kk == 0:
                            pe.wait_ge(xn_ok, 2 + 4)
                            pe.wait_ge(y_taken, 2)
                        transpose_group(2 * KD + kk, xn)

            def ff_bank(ff, j, ch):
                return 4 * (1 - ff) + 2 * j + ch

            def up(ff, j, ch, n, k):
                return product(PS[:, ff_bank(ff, j, ch)], [w[:, n % 2, k] for w in w_hl],
                               [a[:, k, ch * NT:(ch + 1) * NT] for a in act_hl], k == 0, k == KD - 1)

            pe.wait_ge(h_lo, 3 * KD)
            pe.wait_ge(y_taken, NTOK - 1)
            for j in range(2):
                pe.wait_ge(w_split, N_FF + j + 1)
                for k in range(KD):
                    ins = up(0, j, 0, N_FF + j, k)
                    if j == 1 and k >= 5:
                        pe.wait_ge(xn_ok, 2 + NTOK)
                        transpose_group(3 * KD + k - 5, xn)
                ins.then_inc(ff_ready, 1)
            for k in range(3, KD):
                transpose_group(3 * KD + k, xn)
            for j in range(2):
                for k in range(KD):
                    pe.wait_ge(h_lo, 3 * KD + k + 1)
                    ins = up(0, j, 1, N_FF + j, k)
                ins.then_inc(ff_ready, 1)
            pe.wait_ge(y_taken, NTOK)
            for j in range(2):
                pe.wait_ge(w_split, N_FF + 2 + j + 1)
                for ch in range(CH):
                    for k in range(KD):
                        ins = up(1, j, ch, N_FF + 2 + j, k)
                    ins.then_inc(ff_ready, 1)
            with pe.Fori(1, FT // 2) as it:
                for ff in range(2):
                    for j in range(2):
                        n = N_FF + 2 * ff + j
                        pe.wait_ge(w_split, it * 4 + (n + 1))
                        for ch in range(CH):
                            if j == 0 and ch == 0:
                                pe.wait_ge(ff_ok, it * 4 + (2 * ff + 2))
                            for k in range(KD):
                                ins = up(ff, j, ch, n, k)
                            ins.then_inc(ff_ready, 1)

            def down(t, j, first, last):
                return product(PS[:, t], [a[:, j, t * P:(t + 1) * P] for a in ah_hl], [w[:, j] for w in w2_hl], first, last)

            pe.wait_ge(ff_ok, 4 + 2 * FT)
            for half in range(2):
                def operands(it, j):
                    pe.wait_ge(ah_split, it * 2 + (FT * half + j + 1))
                    pe.wait_ge(w2_split, it * 2 + (FT * half + j + 3))

                for j in range(2):
                    operands(0, j)
                    for t in range(NTOK):
                        if half == 1 and j == 0:
                            pe.wait_ge(z_taken, t + 1)
                        ins = down(t, j, j == 0, False)
                        if half == 1 and j == 0 and t == 0:
                            ins.then_inc(ah_used, 1)
                    ins.then_inc(ah_used, 1)
                with pe.Fori(1, FT // 2 - 1) as it:
                    for j in range(2):
                        operands(it, j)
                        for t in range(NTOK):
                            ins = down(t, j, False, False)
                        ins.then_inc(ah_used, 1)
                if half == 0:
                    for j in range(2):
                        operands(FT // 2 - 1, j)
                        for t in range(NTOK):
                            ins = down(t, j, False, j == 1)
                            if j == 1:
                                ins.then_inc(z_ready, 1)
                        if j == 0:
                            ins.then_inc(ah_used, 1)
                else:
                    for j in range(2):
                        operands(FT // 2 - 1, j)
                    for t in range(NTOK):
                        for j in range(2):
                            ins = down(t, j, False, j == 1)
                        ins.then_inc(z_ready, 1)


_INS = ["x", "c", "positions", "w_ada", "b_ada", "g_pre_mix", "g_post_mix", "w_in", "b_f", "sinks", "w_branch_a",
        "w_branch_b", "w_out", "g_pre_ffn", "g_post_ffn", "w_ffn_in", "w_ffn_out"]
_OUT = ((1, 1024, 1024), "float32")


def _inverse_frequencies():
    import numpy as np
    half = np.arange(0, 64, 2, dtype=np.float32) / np.float32(64)
    return np.tile(np.float32(1.0) / (np.float32(10000.0) ** half), 4).reshape(128, 1).astype(np.float32)


def kernel(**inputs):
    import numpy as np
    import concourse.bacc as bacc
    from concourse import mybir as mb
    from concourse.bass_utils import run_bass_kernel_spmd as run

    nc = bacc.Bacc("TRN2", target_bir_lowering=False, num_devices=1, dynamic_dma_scratch_size=1024)
    arrays, args = {}, []

    def give(name, a):
        arrays[f"in_{name}_dram"] = a
        args.append(nc.dram_tensor(f"in_{name}_dram", a.shape, mb.dt.from_np(a.dtype), kind="ExternalInput").ap())

    for name in _INS:
        give(name, np.ascontiguousarray(inputs[name]))
    give("inv_freq", _inverse_frequencies())
    args.append(nc.dram_tensor("out_0_dram", _OUT[0], mb.dt.from_np(np.dtype(_OUT[1])), kind="ExternalOutput").ap())
    hybrid_layer(nc, *args)
    return run(nc, [arrays], core_ids=[0]).results[0]["out_0_dram"]
```
